# Optimizing a Trainium2 kernel written in Bass

```python
import math, functools
import jax, jax.numpy as jnp
from jax import lax
import numpy as np

D_MODEL = 1024
BATCH = 1
SEQ = 128
DEPTH = 1
DEC_BATCH = 1
DEC_SEQ = 1024
PAST_LEN = 256

GRID_W = 64
MIX_WIDTH = D_MODEL
HG_WIDTH = MIX_WIDTH // 2
HG_HEAD_DIM = 128
HG_HEADS = HG_WIDTH // HG_HEAD_DIM
ATT_WIDTH = MIX_WIDTH - HG_WIDTH
HEAD_DIM = 64
N_HEADS = ATT_WIDTH // HEAD_DIM
N_KV_HEADS = 2
KV_WIDTH = N_KV_HEADS * HEAD_DIM
IN_WIDTH = 5 * HG_WIDTH + ATT_WIDTH + 2 * KV_WIDTH
D_FF = 128 * ((8 * D_MODEL // 3 + 127) // 128)
CHUNK = 16
Q_BLOCK = 128
ROPE_THETA = 10000.0
N_MOD = 9
ALPHA = (2.0 * DEPTH) ** 0.25
BETA = (8.0 * DEPTH) ** -0.25
LN_EPS = 1e-6
RMS_EPS = 1e-6
f32 = jnp.float32

kernel_name = "hymba_hgrn2_gqa_macaron_deepnorm_prefix_dit_step"

def layer_norm(x, g, b):
    xf = x.astype(f32)
    mu = jnp.mean(xf, -1, keepdims=True)
    var = jnp.mean(jnp.square(xf - mu), -1, keepdims=True)
    return ((xf - mu) * lax.rsqrt(var + LN_EPS) * g + b).astype(x.dtype)

def rms_norm(x, g):
    xf = x.astype(f32)
    return (xf * lax.rsqrt(jnp.mean(xf * xf, -1, keepdims=True) + RMS_EPS) * g).astype(x.dtype)

def modulation(cvec, w_mod, b_mod):
    m = jax.nn.silu(cvec) @ w_mod + b_mod
    m = m.reshape(cvec.shape[:-1] + (N_MOD, D_MODEL))
    return [m[..., i, None, :] for i in range(N_MOD)]

def swiglu(h, w_up, w_down):
    a, u = jnp.split(h @ w_up, 2, axis=-1)
    return (jax.nn.silu(a) * u) @ w_down

def split_in(z):
    cuts = [HG_WIDTH, 2 * HG_WIDTH, 3 * HG_WIDTH, 4 * HG_WIDTH, 5 * HG_WIDTH,
            5 * HG_WIDTH + ATT_WIDTH, 5 * HG_WIDTH + ATT_WIDTH + KV_WIDTH]
    return jnp.split(z, cuts, axis=-1)

def axial_rope_angles(n_tokens):
    rows = n_tokens // GRID_W
    t_row = jnp.repeat(jnp.arange(rows), GRID_W).astype(f32)
    t_col = jnp.tile(jnp.arange(GRID_W), rows).astype(f32)
    half = HEAD_DIM // 2
    inv = ROPE_THETA ** (-jnp.arange(0, half, 2, dtype=f32) / half)
    return t_row[:, None] * inv, t_col[:, None] * inv

def rope_rotate(x, ang):
    x1, x2 = jnp.split(x, 2, axis=-1)
    cos = jnp.cos(ang)[:, None, :]
    sin = jnp.sin(ang)[:, None, :]
    return jnp.concatenate([x1 * cos - x2 * sin, x1 * sin + x2 * cos], axis=-1)

def apply_axial_rope(x, ang_row, ang_col):
    xr, xc = jnp.split(x.astype(f32), 2, axis=-1)
    return jnp.concatenate([rope_rotate(xr, ang_row), rope_rotate(xc, ang_col)], -1).astype(x.dtype)

def block_attention(q, k, v):
    b, lq, h, dh = q.shape
    nb = lq // Q_BLOCK
    grp = h // N_KV_HEADS
    qb = q.reshape(b, nb, Q_BLOCK, N_KV_HEADS, grp, dh).transpose(1, 0, 2, 3, 4, 5)
    scale = dh ** -0.5

    def one_block(qi):
        s = jnp.einsum("bqkgd,bskd->bkgqs", qi, k).astype(f32) * scale
        p = jax.nn.softmax(s, axis=-1).astype(v.dtype)
        return jnp.einsum("bkgqs,bskd->bqkgd", p, v)

    o = lax.map(one_block, qb)
    return o.transpose(1, 0, 2, 3, 4, 5).reshape(b, lq, h * dh)

def hgrn2_scan(q, k, log_f, v, s0):
    b, l, h, _ = q.shape
    n = l // CHUNK
    rs = lambda t: t.reshape(b, n, CHUNK, h, t.shape[-1])
    q, k, log_f, v = rs(q), rs(k), rs(log_f), rs(v)
    g = jnp.cumsum(log_f, axis=2)
    g_last = g[:, :, -1]
    mask = jnp.tril(jnp.ones((CHUNK, CHUNK), dtype=bool))
    rel = g[:, :, :, None] - g[:, :, None, :]
    decay = jnp.exp(jnp.where(mask[:, :, None, None], rel, -jnp.inf))
    a = jnp.einsum("bnihk,bnjhk,bnijhk->bnhij", q, k, decay)
    o_intra = jnp.einsum("bnhij,bnjhv->bnihv", a, v)
    k_end = k * jnp.exp(g_last[:, :, None] - g)
    upd = jnp.einsum("bnjhk,bnjhv->bnhkv", k_end, v)
    tot = jnp.exp(g_last)

    def step(s, inp):
        t, u = inp
        return t[..., None] * s + u, s

    s_fin, s_prev = lax.scan(step, s0, (jnp.moveaxis(tot, 1, 0), jnp.moveaxis(upd, 1, 0)))
    s_prev = jnp.moveaxis(s_prev, 0, 1)
    o_inter = jnp.einsum("bnihk,bnhkv->bnihv", q * jnp.exp(g), s_prev)
    return (o_intra + o_inter).reshape(b, l, h, -1), s_fin

def hgrn2_mixer(hq, hi, hf_fwd, hf_bwd, hgate, lb_fwd, lb_bwd, norm_g, s_fwd0, s_bwd0):
    b, l, _ = hq.shape
    heads = lambda t: t.reshape(b, l, HG_HEADS, HG_HEAD_DIM)
    q = heads(jax.nn.silu(hq.astype(f32)))
    v = heads(hi.astype(f32))

    def direction(hf, lb, s0, flip):
        f = lb + (1.0 - lb) * jax.nn.sigmoid(hf.astype(f32))
        args = (q, heads(1.0 - f), heads(jnp.log(f)), v)
        if flip:
            args = tuple(t[:, ::-1] for t in args)
        o, s = hgrn2_scan(*args, s0.astype(f32))
        if flip:
            o = o[:, ::-1]
        return o, s

    o_f, s_f = direction(hf_fwd, lb_fwd, s_fwd0, False)
    o_b, s_b = direction(hf_bwd, lb_bwd, s_bwd0, True)
    o = rms_norm(o_f + o_b, norm_g.reshape(HG_HEADS, HG_HEAD_DIM)).reshape(b, l, HG_WIDTH)
    o = o * jax.nn.silu(hgate.astype(f32))
    return o.astype(hq.dtype), s_f, s_b

def attn_proj(aq, ak, av, q_g, k_g):
    b, l, _ = aq.shape
    q = rms_norm(aq.reshape(b, l, N_HEADS, HEAD_DIM), q_g)
    k = rms_norm(ak.reshape(b, l, N_KV_HEADS, HEAD_DIM), k_g)
    v = av.reshape(b, l, N_KV_HEADS, HEAD_DIM)
    return q, k, v

def mixer_context(h, *, w_in, w_out, q_g, k_g, hg_g, lb_f, lb_b):
    hq, hi, hff, hfb, hgate, aq, ak, av = split_in(h @ w_in)
    s_zero = jnp.zeros((h.shape[0], HG_HEADS, HG_HEAD_DIM, HG_HEAD_DIM), f32)
    o_hg, s_f, s_b = hgrn2_mixer(hq, hi, hff, hfb, hgate, lb_f, lb_b, hg_g, s_zero, s_zero)
    q, k, v = attn_proj(aq, ak, av, q_g, k_g)
    o_att = block_attention(q, k, v)
    y = jnp.concatenate([o_hg, o_att.astype(o_hg.dtype)], axis=-1) @ w_out
    return y, (k, v, s_f, s_b)

def mixer_latent(h, *, k_ctx, v_ctx, s_f0, s_b0, w_in, w_out, q_g, k_g, hg_g, lb_f, lb_b):
    hq, hi, hff, hfb, hgate, aq, ak, av = split_in(h @ w_in)
    o_hg, _, _ = hgrn2_mixer(hq, hi, hff, hfb, hgate, lb_f, lb_b, hg_g, s_f0, s_b0)
    q, k, v = attn_proj(aq, ak, av, q_g, k_g)
    ang_row, ang_col = axial_rope_angles(h.shape[1])
    q = apply_axial_rope(q, ang_row, ang_col)
    k = apply_axial_rope(k, ang_row, ang_col)
    k_all = jnp.concatenate([k_ctx.astype(k.dtype), k], axis=1)
    v_all = jnp.concatenate([v_ctx.astype(v.dtype), v], axis=1)
    o_att = block_attention(q, k_all, v_all)
    y = jnp.concatenate([o_hg, o_att.astype(o_hg.dtype)], axis=-1) @ w_out
    return y, ()

def trunk_layer(x, cvec, mixer, w_mod, b_mod, w_f1_in, w_f1_out, w_f2_in, w_f2_out, ln_g, ln_b):
    sh1, sc1, g1, sh2, sc2, g2, sh3, sc3, g3 = modulation(cvec, w_mod, b_mod)
    x = layer_norm(ALPHA * x + 0.5 * g1 * swiglu(x * (1.0 + sc1) + sh1, w_f1_in, w_f1_out), ln_g[0], ln_b[0])
    y, aux = mixer(x * (1.0 + sc2) + sh2)
    x = layer_norm(ALPHA * x + g2 * y, ln_g[1], ln_b[1])
    x = layer_norm(ALPHA * x + 0.5 * g3 * swiglu(x * (1.0 + sc3) + sh3, w_f2_in, w_f2_out), ln_g[2], ln_b[2])
    return x, aux

def setup_inputs(seed: int = 0) -> dict:
    key = jax.random.key(seed)
    ks = jax.random.split(key, 24)
    nrm = lambda k, shape, scale: scale * jax.random.normal(k, shape, f32)
    d = D_MODEL
    col_scale = jnp.ones((IN_WIDTH,), f32)
    col_scale = col_scale.at[HG_WIDTH:2 * HG_WIDTH].set(BETA).at[IN_WIDTH - KV_WIDTH:].set(BETA)
    return {
        "x_prompt": nrm(ks[0], (BATCH, SEQ, d), 1.0),
        "x_sample": nrm(ks[1], (DEC_BATCH, DEC_SEQ, d), 1.0),
        "cache_k": nrm(ks[2], (DEC_BATCH, DEPTH, PAST_LEN, N_KV_HEADS, HEAD_DIM), 1.0),
        "cache_v": nrm(ks[3], (DEC_BATCH, DEPTH, PAST_LEN, N_KV_HEADS, HEAD_DIM), 0.5),
        "state_hgrn_fwd": nrm(ks[4], (DEC_BATCH, DEPTH, HG_HEADS, HG_HEAD_DIM, HG_HEAD_DIM), 0.5),
        "state_hgrn_bwd": nrm(ks[5], (DEC_BATCH, DEPTH, HG_HEADS, HG_HEAD_DIM, HG_HEAD_DIM), 0.5),
        "c": nrm(ks[6], (DEC_BATCH, d), 1.0),
        "c_ctx": nrm(ks[7], (d,), 1.0),
        "w_mod": nrm(ks[8], (DEPTH, d, N_MOD * d), 0.5 * d ** -0.5),
        "b_mod": nrm(ks[9], (DEPTH, N_MOD * d), 0.02),
        "w_ffn1_in": nrm(ks[10], (DEPTH, d, 2 * D_FF), BETA * d ** -0.5),
        "w_ffn1_out": nrm(ks[11], (DEPTH, D_FF, d), BETA * D_FF ** -0.5),
        "w_ffn2_in": nrm(ks[12], (DEPTH, d, 2 * D_FF), BETA * d ** -0.5),
        "w_ffn2_out": nrm(ks[13], (DEPTH, D_FF, d), BETA * D_FF ** -0.5),
        "w_in": nrm(ks[14], (DEPTH, d, IN_WIDTH), d ** -0.5) * col_scale,
        "w_out": nrm(ks[15], (DEPTH, MIX_WIDTH, d), BETA * MIX_WIDTH ** -0.5),
        "q_norm_g": 1.0 + nrm(ks[16], (DEPTH, HEAD_DIM), 0.05),
        "k_norm_g": 1.0 + nrm(ks[17], (DEPTH, HEAD_DIM), 0.05),
        "hg_norm_g": 1.0 + nrm(ks[18], (DEPTH, HG_WIDTH), 0.05),
        "lb_logits_fwd": nrm(ks[19], (DEPTH + 1, HG_WIDTH), 0.5),
        "lb_logits_bwd": nrm(ks[20], (DEPTH + 1, HG_WIDTH), 0.5),
        "ln_g": 1.0 + nrm(ks[21], (DEPTH, 3, d), 0.05),
        "ln_b": nrm(ks[22], (DEPTH, 3, d), 0.02),
    }

def reference(x_prompt, x_sample, cache_k, cache_v, state_hgrn_fwd, state_hgrn_bwd, c, c_ctx,
              w_mod, b_mod, w_ffn1_in, w_ffn1_out, w_ffn2_in, w_ffn2_out, w_in, w_out,
              q_norm_g, k_norm_g, hg_norm_g, lb_logits_fwd, lb_logits_bwd, ln_g, ln_b):
    lb_f_all = jnp.cumsum(jax.nn.softmax(lb_logits_fwd.astype(f32), axis=0), axis=0)
    lb_b_all = jnp.cumsum(jax.nn.softmax(lb_logits_bwd.astype(f32), axis=0), axis=0)

    y_prompt = x_prompt
    ks_l, vs_l, sf_l, sb_l = [], [], [], []
    for l in range(DEPTH):
        mix = functools.partial(mixer_context, w_in=w_in[l], w_out=w_out[l], q_g=q_norm_g[l],
                                k_g=k_norm_g[l], hg_g=hg_norm_g[l], lb_f=lb_f_all[l], lb_b=lb_b_all[l])
        y_prompt, (k_l, v_l, s_f, s_b) = trunk_layer(
            y_prompt, c_ctx, mix, w_mod[l], b_mod[l], w_ffn1_in[l], w_ffn1_out[l],
            w_ffn2_in[l], w_ffn2_out[l], ln_g[l], ln_b[l])
        ks_l.append(k_l)
        vs_l.append(v_l)
        sf_l.append(s_f)
        sb_l.append(s_b)
    new_cache_k = jnp.stack(ks_l, axis=1)
    new_cache_v = jnp.stack(vs_l, axis=1)
    new_state_fwd = jnp.stack(sf_l, axis=1)
    new_state_bwd = jnp.stack(sb_l, axis=1)

    y_sample = x_sample
    for l in range(DEPTH):
        mix = functools.partial(mixer_latent, k_ctx=cache_k[:, l], v_ctx=cache_v[:, l],
                                s_f0=state_hgrn_fwd[:, l], s_b0=state_hgrn_bwd[:, l],
                                w_in=w_in[l], w_out=w_out[l], q_g=q_norm_g[l], k_g=k_norm_g[l],
                                hg_g=hg_norm_g[l], lb_f=lb_f_all[l], lb_b=lb_b_all[l])
        y_sample, _ = trunk_layer(
            y_sample, c, mix, w_mod[l], b_mod[l], w_ffn1_in[l], w_ffn1_out[l],
            w_ffn2_in[l], w_ffn2_out[l], ln_g[l], ln_b[l])

    return (y_prompt, y_sample, new_cache_k, new_cache_v, new_state_fwd, new_state_bwd)


_drawn_inputs = setup_inputs


def setup_inputs(seed=0):
    import zlib

    import numpy as np

    out = dict(_drawn_inputs(seed))
    spreads = {}
    factors = {'cache_k': 8.0,
     'cache_v': 8.0,
     'state_hgrn_fwd': 8.0,
     'state_hgrn_bwd': 8.0,
     'w_ffn1_in': 3.286,
     'w_ffn1_out': 3.288,
     'w_ffn2_in': 3.384,
     'w_ffn2_out': 3.376,
     'q_norm_g': 8.0,
     'hg_norm_g': 8.0}
    for name, (base, spread) in spreads.items():
        noise = np.random.default_rng([zlib.crc32(name.encode()), seed]).standard_normal(out[name].shape)
        drawn = base * np.exp(spread * noise) if base else spread * noise
        out[name] = __import__('jax').numpy.asarray(drawn.astype(out[name].dtype))
    for name, factor in factors.items():
        out[name] = (out[name] * factor).astype(out[name].dtype)
    return out
```

```python
from contextlib import ExitStack

import numpy as np
import concourse.bass as bass
from concourse import mybir

ALU = mybir.AluOpType
ACT = mybir.ActivationFunctionType
F32 = mybir.dt.float32
F32R = mybir.dt.float32r
AX_X = mybir.AxisListType.X

P = 128
D = 1024
KT = D // P
N_LAT, N_CTX = 1024, 128
TOK = N_LAT + N_CTX
NT = TOK // P
CTX_T = N_LAT // P
CH = 384
NCH = TOK // CH
TPC = CH // P
FF = 2816
NB = FF // P
GB = 2
NG = NB // GB
HGW = 512
HGH = 4
NH, NKV, DH = 8, 2, 64
QW, KVW = NH * DH, NKV * DH
IN_W = 5 * HGW + QW + 2 * KVW
PAST = 256
GRID_W = 64
N_MOD = 9
ALPHA = 2.0 ** 0.25
EPS = 1e-6
SCAN = 32
NSC = TOK // SCAN
LSC = N_LAT // SCAN

C_BMOD, C_LNG, C_LNB, C_C, C_CCTX, C_LBF, C_LBB, C_HGN, C_END = 0, 72, 96, 120, 128, 136, 144, 152, 156
PASSES = ((0, 0), (0, 1), (1, 0))


class Plan:

    def __init__(self, nc, base):
        self.nc, self.at = nc, base

    def __call__(self, name, shape, dt=F32):
        size = int(np.prod(shape[1:])) * 4
        t = self.nc.alloc_sbuf_tensor_at(name, shape, dt, offset=self.at)
        self.at += (size + 31) // 32 * 32
        assert self.at <= self.nc.sbuf_usable_end, (name, self.at, self.nc.sbuf_usable_end)
        return t


class Chain:

    def __init__(self, eng, sem):
        self.eng, self.sem, self.n = eng, sem, 0

    def __call__(self, ins):
        self.n += 1
        ins.then_inc(self.sem, 1)
        self.eng.wait_ge(self.sem, self.n)


class LoopChain(Chain):

    def begin(self, i, per):
        self.per, self.n, self.base = per, 0, i * per

    def __call__(self, ins):
        self.n += 1
        ins.then_inc(self.sem, 1)
        self.eng.wait_ge(self.sem, self.base + self.n)

    def end(self):
        assert self.n == self.per, self.n


class Feed:

    def __init__(self, K, ctx, nc, tag, src, tmp, banks, scale_i, shift_i):
        self.K, self.nc, self.src, self.tmp, self.banks = K, nc, src, tmp, banks
        self.scale_i, self.shift_i = scale_i, shift_i
        sem = lambda n: K.semaphore(f"{tag}_{n}")
        self.turned, self.affine, self.hi, self.lo = sem("turned"), sem("affine"), sem("feed_hi"), sem("feed_lo")

    def turn(self, pe, wait_chunk):
        for c in range(NCH):
            wait_chunk(c)
            for k in range(KT):
                n = c * KT + k
                if n >= 4:
                    pe.wait_ge(self.affine, n - 3)
                for j in range(TPC):
                    t = c * TPC + j
                    last = self.nc.tensor.transpose(self.banks[n % 4][:, j * P:(j + 1) * P],
                                                    self.src[:, t, k * P:(k + 1) * P], self.K.ident[:])
                last.then_inc(self.turned, 1)

    def scale(self, act):
        K, nc = self.K, self.nc
        for c in range(NCH):
            for k in range(KT):
                n = c * KT + k
                act.wait_ge(self.turned, n + 1)
                if n >= 2:
                    act.wait_ge(self.lo, n - 1)
                cuts = [(0, CH, 0)] if c < NCH - 1 else [(0, CH - P, 0), (CH - P, CH, 1)]
                for a, b, v in cuts:
                    last = nc.scalar.activation(self.tmp[n % 2][:, a:b], self.banks[n % 4][:, a:b], ACT.Identity,
                                                bias=K.mod[:, self.shift_i * KT + k, v:v + 1],
                                                scale=K.mod[:, self.scale_i * KT + k, v:v + 1])
                last.then_inc(self.affine, 1)
                act.wait_ge(self.affine, n + 1)
                nc.scalar.activation(K.A[0][:, k, c * CH:(c + 1) * CH], self.tmp[n % 2][:], ACT.Copy).then_inc(self.hi, 1)

    def rest(self, dve, c):
        K, nc = self.K, self.nc
        for k in range(KT):
            n = c * KT + k
            dve.wait_ge(self.hi, n + 1)
            nc.vector.tensor_tensor(K.A[1][:, k, c * CH:(c + 1) * CH], self.tmp[n % 2][:],
                                    K.A[0][:, k, c * CH:(c + 1) * CH].bitcast(F32), ALU.subtract).then_inc(self.lo, 1)


class Norm:

    def __init__(self, K, ctx, nc, tag, place, ln_i, gate_i, res_src, out_dst, gB, bB, xo):
        self.K, self.nc, self.ln_i, self.gate_i = K, nc, ln_i, gate_i
        self.res_src, self.out_dst, self.gB, self.bB, self.xo = res_src, out_dst, gB, bB, xo
        sem = lambda n: K.semaphore(f"{tag}_{n}")
        self.gate = place(f"{tag}_gate_rows", [P, 2, D])
        self.xs = place(f"{tag}_residual", [P, D])
        self.st = place(f"{tag}_stats", [P, 2, 6])
        self.mv = place(f"{tag}_meanvar", [P, NT, 2])
        self.rs = place(f"{tag}_rstd", [P, NT])
        self.half = place(f"{tag}_minus_half", [P, 1])
        self.gates, self.rows = sem("gate_rows_loaded"), sem("ln_rows_loaded")
        self.res, self.res_used = sem("residual_loaded"), sem("residual_used")
        self.chain, self.bn, self.rstd, self.z = sem("norm_chain"), sem("bn_done"), sem("rstd_done"), sem("z_done")
        self.pool_chain, self.xo_done, self.stored = sem("pool_chain"), sem("xo_done"), sem("x_stored")

    def load(self, sp, affine_free):
        K = self.K
        for v in range(2):
            sp.dma_start(self.gate[:, v, :], K.mod_rows[v:v + 1, self.gate_i * D:(self.gate_i + 1) * D]
                         .broadcast_to([P, D])).then_inc(self.gates, 16)
        sp.dma_start(self.xs[:], self.res_src(0)).then_inc(self.res, 16)
        affine_free()
        sp.dma_start(self.gB, K.ln_g[self.ln_i:self.ln_i + 1, :].broadcast_to([P, D])).then_inc(self.rows, 16)
        sp.dma_start(self.bB, K.ln_b[self.ln_i:self.ln_i + 1, :].broadcast_to([P, D])).then_inc(self.rows, 16)
        for t in range(1, NT + 2):
            if t < NT:
                sp.wait_ge(self.res_used, t)
                sp.dma_start(self.xs[:], self.res_src(t)).then_inc(self.res, 16)
            if t >= 2:
                sp.wait_ge(self.xo_done, t - 1)
                sp.dma_start(self.out_dst(t - 2), self.xo).then_inc(self.stored, 16)
        sp.wait_ge(self.stored, 16 * NT)

    def start(self, dve):
        self.link = Chain(dve, self.chain)

    def sums(self, dve, t, Y, src=None, freed=None):
        nc, v = self.nc, int(t == CTX_T)
        if t == 0:
            dve.wait_ge(self.gates, 32)
        ins = nc.vector.tensor_tensor(Y[:, t, :], Y[:, t, :] if src is None else src, self.gate[:, v, :], ALU.mult)
        if freed is not None:
            ins.then_inc(freed, 1)
            dve.wait_ge(freed, t + 1)
        else:
            self.link(ins)
        dve.wait_ge(self.res, 16 * (t + 1))
        nc.vector.scalar_tensor_tensor(Y[:, t, :], self.xs[:], ALPHA, Y[:, t, :], ALU.mult, ALU.add).then_inc(self.res_used, 1)
        dve.wait_ge(self.res_used, t + 1)
        if t:
            dve.wait_ge(self.bn, t)
        for h in range(2):
            self.link(nc.vector.bn_stats(self.st[:, h, :], Y[:, t, h * 512:(h + 1) * 512]))
        nc.vector.bn_aggr(self.mv[:, t, :], self.st[:]).then_inc(self.bn, 1)

    def unit(self, dve, t, Y):
        dve.wait_ge(self.bn, t + 1)
        dve.wait_ge(self.rstd, t + 1)
        self.nc.vector.tensor_scalar(Y[:, t, :], Y[:, t, :], self.mv[:, t, 0:1], self.rs[:, t:t + 1],
                                     ALU.subtract, ALU.mult).then_inc(self.z, 1)

    def pool(self, gp, Y, xo_free=None):
        nc = self.nc
        link = Chain(gp, self.pool_chain)
        link(nc.gpsimd.memset(self.half[:], -0.5))

        def rstd(t):
            gp.wait_ge(self.bn, t + 1)
            link(nc.gpsimd.tensor_scalar(self.rs[:, t:t + 1], self.mv[:, t, 1:2], EPS, None, ALU.add))
            nc.gpsimd.tensor_tensor(self.rs[:, t:t + 1], self.rs[:, t:t + 1], self.half[:], ALU.pow).then_inc(self.rstd, 1)

        rstd(0)
        for t in range(NT):
            if t + 1 < NT:
                rstd(t + 1)
            if t == 0:
                gp.wait_ge(self.rows, 32)
                if xo_free is not None:
                    xo_free(gp)
            else:
                gp.wait_ge(self.stored, 16 * t)
            gp.wait_ge(self.z, t + 1)
            link(nc.gpsimd.tensor_tensor(self.xo, Y[:, t, :], self.gB, ALU.mult))
            nc.gpsimd.tensor_tensor(self.xo, self.xo, self.bB, ALU.add).then_inc(self.xo_done, 1)


def modulation_phase(nc, K, place, banks):
    with ExitStack() as ctx:
        sem = lambda n: K.semaphore(f"mod_{n}")
        rows1 = place("param_rows_1", [P, P])
        rows2 = place("param_rows_2", [C_END - P, P])
        silu = place("silu_cond", [P, KT, 2])
        wbuf = [place(f"w_mod_{i}", [P, KT, D]) for i in range(2)]
        tmp = [place(f"mod_tmp_{i}", [P, CH]) for i in range(2)]
        bounce = place("mod_bounce", [P, 2, P])
        ncol = place("mod_scratch", [P, 16, 2])
        feed = Feed(K, ctx, nc, "mod", K.Y, tmp, [banks[i] for i in range(4)], 1, 0)
        p_col, p_mod = banks[4], banks[5]
        rows_in, ident_ok, cols_t, cols_ok, silu_ok = (sem(n) for n in ("rows_in", "ident_ok", "cols_turned", "cols_ok", "silu_ok"))
        w_in = [sem("w_in_even"), sem("w_in_odd")]
        w_used, chain, mod_ok = (sem(n) for n in ("w_used", "chain", "mod_ok"))
        x_in, pool_chain, r_turned, r_ok, r_out = (sem(n) for n in ("x_in", "pool_chain", "rows_turned", "rows_ok", "rows_out"))
        w_mod = K.w_mod[0].rearrange("(k p) n -> p k n", p=P)
        block = ctx.enter_context(nc.Block())

        @block.sync
        def _(sp):
            vec = lambda a, n: a.rearrange("(j p) -> j p", p=P) if n else a
            sp.dma_start(rows1[C_BMOD:C_LNG, :], K.b_mod[0].rearrange("(j p) -> j p", p=P)).then_inc(rows_in, 16)
            sp.dma_start(rows1[C_LNG:C_LNB, :], K.ln_g.rearrange("l (j p) -> (l j) p", p=P)).then_inc(rows_in, 16)
            sp.dma_start(rows1[C_LNB:C_C, :], K.ln_b.rearrange("l (j p) -> (l j) p", p=P)).then_inc(rows_in, 16)
            sp.dma_start(rows1[C_C:C_CCTX, :], K.c[0].rearrange("(j p) -> j p", p=P)).then_inc(rows_in, 16)
            sp.dma_start(rows2[0:C_LBF - P, :], K.c_ctx.rearrange("(j p) -> j p", p=P)).then_inc(rows_in, 16)
            sp.dma_start(rows2[C_LBF - P:C_LBB - P, :], K.lb_f.rearrange("l (j p) -> (l j) p", p=P)).then_inc(rows_in, 16)
            sp.dma_start(rows2[C_LBB - P:C_HGN - P, :], K.lb_b.rearrange("l (j p) -> (l j) p", p=P)).then_inc(rows_in, 16)
            sp.dma_start(rows2[C_HGN - P:C_END - P, :], K.hg_g[0].rearrange("(j p) -> j p", p=P)).then_inc(rows_in, 16)
            for m in range(N_MOD):
                if m >= 2:
                    sp.wait_ge(w_used, m - 1)
                sp.dma_start(wbuf[m % 2][:], w_mod[:, :, m * D:(m + 1) * D]).then_inc(w_in[m % 2], 16)
                if m == 1:
                    for t in range(NT):
                        sp.dma_start(K.Y[:, t, :], K.x_rows(t)).then_inc(x_in, 16)
            for v in range(2):
                sp.wait_ge(r_ok, v + 1)
                sp.dma_start(K.mod_rows[v].rearrange("(j p) -> j p", p=P), bounce[0:72, v, :]).then_inc(r_out, 16)
            sp.wait_ge(r_out, 32)

        @block.gpsimd
        def _(gp):
            link = Chain(gp, pool_chain)
            link(nc.gpsimd.memset(K.ident[:], 0.0))
            nc.gpsimd.affine_select(out=K.ident[:], in_=K.ident[:], compare_op=ALU.not_equal, fill=1.0, base=0,
                                    pattern=[[-1, P]], channel_multiplier=1).then_inc(ident_ok, 1)

        @block.tensor
        def _(pe):
            pe.wait_ge(ident_ok, 1)
            pe.wait_ge(rows_in, 128)
            nc.tensor.transpose(p_col[:, 0:P], rows1[:], K.ident[:])
            nc.tensor.transpose(p_col[:, P:C_END], rows2[:], K.ident[0:C_END - P, 0:C_END - P]).then_inc(cols_t, 1)
            pe.wait_ge(silu_ok, 1)
            for m in range(N_MOD):
                pe.wait_ge(w_in[m % 2], 16 * (m // 2 + 1))
                for j in range(KT):
                    col = 2 * (m * KT + j)
                    for k in range(KT):
                        last = nc.tensor.matmul(p_mod[:, col:col + 2], wbuf[m % 2][:, k, j * P:(j + 1) * P],
                                                silu[:, k, :], start=(k == 0), stop=(k == KT - 1))
                last.then_inc(w_used, 1)
            pe.wait_ge(mod_ok, 1)
            for v in range(2):
                nc.tensor.transpose(p_col[0:72, v * P:(v + 1) * P], K.mod[:, :, v], K.ident[:]).then_inc(r_turned, 1)
            feed.turn(pe, lambda c: pe.wait_ge(x_in, 16 * NT) if c == 0 else None)

        @block.scalar
        def _(act):
            act.wait_ge(cols_ok, 1)
            nc.scalar.activation(silu[:].rearrange("p k v -> p v k"),
                                 K.cols[:, C_C:C_LBF].rearrange("p (v k) -> p v k", v=2), ACT.Silu).then_inc(silu_ok, 1)
            act.wait_ge(mod_ok, 1)
            for v in range(2):
                act.wait_ge(r_turned, 2)
                nc.scalar.copy(bounce[0:72, v, :], p_col[0:72, v * P:(v + 1) * P]).then_inc(r_ok, 1)
            feed.scale(act)

        @block.vector
        def _(dve):
            link = Chain(dve, chain)
            dve.wait_ge(cols_t, 1)
            nc.vector.tensor_copy(K.cols[:], p_col[:, 0:C_END]).then_inc(cols_ok, 1)
            dve.wait_ge(cols_ok, 1)
            for i, c0 in enumerate((C_LBF, C_LBB)):
                link(nc.vector.tensor_tensor(K.lbd[:, i, :], K.cols[:, c0:c0 + HGH], K.cols[:, c0 + HGH:c0 + 2 * HGH], ALU.subtract))
            dve.wait_ge(w_used, N_MOD)
            M = K.mod
            link(nc.vector.tensor_tensor(M[:], p_mod[:, 0:144].rearrange("p (j v) -> p j v", v=2),
                                         K.cols[:, 0:72].unsqueeze(2).broadcast_to([P, 72, 2]), ALU.add))
            grp = lambda i: M[:, i * KT:(i + 1) * KT, :]
            for i in (1, 4, 7):
                link(nc.vector.tensor_scalar(grp(i), grp(i), 1.0, None, ALU.add))
            for i in (2, 8):
                link(nc.vector.tensor_scalar(grp(i), grp(i), 0.5, None, ALU.mult))
            for l, (ish, isc) in enumerate(((3, 4), (6, 7))):
                g = K.cols[:, C_LNG + l * KT:C_LNG + (l + 1) * KT].unsqueeze(2).broadcast_to([P, KT, 2])
                b = K.cols[:, C_LNB + l * KT:C_LNB + (l + 1) * KT].unsqueeze(2).broadcast_to([P, KT, 2])
                link(nc.vector.tensor_tensor(ncol[:, 0:KT, :], grp(isc), b, ALU.mult))
                link(nc.vector.tensor_tensor(grp(ish), grp(ish), ncol[:, 0:KT, :], ALU.add))
                link(nc.vector.tensor_tensor(grp(isc), grp(isc), g, ALU.mult))
            nc.vector.memset(ncol[:, 0:1, 0:1], 0.0).then_inc(mod_ok, 1)
            for c in range(NCH):
                feed.rest(dve, c)


def ffn_phase(nc, K, place, banks, tag, w_in, w_out, res_src, out_dst, gate_i, ln_i, feed_i):
    with ExitStack() as ctx:
        sem = lambda n: K.semaphore(f"{tag}_{n}")
        Y = K.Y
        win = [[place(f"{tag}_win_{s}_{x}", [P, 2, KT, P], F32R) for x in ("hi", "lo")] for s in range(2)]
        raw_at = place.at
        wraw = place(f"{tag}_win_raw", [P, 2, KT, P])
        gB = nc.alloc_sbuf_tensor_at(f"{tag}_ln_g_rows", [P, D], F32, offset=raw_at)
        bB = nc.alloc_sbuf_tensor_at(f"{tag}_ln_b_rows", [P, D], F32, offset=raw_at + 4 * D)
        wout = [place(f"{tag}_wout_{x}", [P, GB, D], F32R) for x in ("hi", "lo")]
        out_at = place.at
        oraw = place(f"{tag}_wout_raw", [P, D])
        xo = nc.alloc_sbuf_tensor_at(f"{tag}_x_row", [P, D], F32, offset=out_at)
        h = [place(f"{tag}_h_{x}", [P, GB, TOK], F32R) for x in ("hi", "lo")]
        sa = [place(f"{tag}_silu_{i}", [P, CH]) for i in range(2)]
        hf = place(f"{tag}_h", [P, CH])
        norm = Norm(K, ctx, nc, tag, place, ln_i, gate_i, res_src, out_dst, gB[:], bB[:], xo[:])
        feed = None
        if feed_i is not None:
            feed = Feed(K, ctx, nc, tag, Y, sa, banks[0:4], *feed_i)
        pa, pu = banks[0:2], banks[2:4]
        py = K.wide[2:4]
        raw_in, in_hi, in_lo = sem("win_loaded"), sem("win_hi"), sem("win_lo")
        raw_out, out_hi, out_lo = sem("wout_loaded"), sem("wout_hi"), sem("wout_lo")
        au, silu, hprod, h_hi, h_lo = sem("au_ready"), sem("silu_done"), sem("h_done"), sem("h_hi"), sem("h_lo")
        y_ready, y_added, y_zero = sem("y_ready"), sem("y_added"), sem("y_zeroed")
        wi_v = w_in[0].rearrange("(k p) (s n) -> p s k n", p=P, s=2)
        wo_v = w_out[0].rearrange("(b p) n -> p b n", p=P)
        block = ctx.enter_context(nc.Block())

        @block.sync
        def _(sp):
            def load_in(blk):
                for s in range(2):
                    sp.dma_start(wraw[:, s], wi_v[:, s, :, bass.ds(blk * P, P)]).then_inc(raw_in, 16)

            load_in(0)

            def group(i, last):
                for b in range(GB):
                    blk = i * GB + b
                    if not (last and b == GB - 1):
                        sp.wait_ge(in_lo, blk + 1)
                        load_in(blk + 1)
                    sp.wait_ge(out_lo, blk + 1)
                    sp.dma_start(oraw[:], wo_v[:, bass.ds(blk, 1), :]).then_inc(raw_out, 16)

            with sp.Fori(0, NG - 1, 1) as i:
                group(i, False)
            group(NG - 1, True)
            norm.load(sp, lambda: sp.wait_ge(in_lo, NB))

        @block.tensor
        def _(pe):
            def group(i):
                for b in range(GB):
                    blk = i * GB + b
                    for c in range(NCH):
                        u = i * (GB * NCH) + b * NCH + c
                        if c == 0:
                            pe.wait_ge(in_lo, blk + 1)
                        pe.wait_ge(hprod, u + 1)
                        s = (b * NCH + c) % 2
                        for half, bank in ((0, pa[s]), (1, pu[s])):
                            n = 0
                            for k in range(KT):
                                for w, a in PASSES:
                                    last = nc.tensor.matmul(bank[:, 0:CH], win[b][w][:, half, k, :],
                                                            K.A[a][:, k, c * CH:(c + 1) * CH],
                                                            start=(n == 0), stop=(n == 3 * KT - 1))
                                    n += 1
                        last.then_inc(au, 1)
                pe.wait_ge(out_lo, i * GB + GB + 1)
                for t in range(NT):
                    pe.wait_ge(h_lo, i * (GB * NCH) + NCH + t // TPC + 2)
                    pe.wait_ge(y_added, i * NT + (2 if t == 0 else t + 1))
                    n = 0
                    for b in range(GB):
                        for a, w in PASSES:
                            for half in range(2):
                                last = nc.tensor.matmul(py[t % 2][:, half * 512:(half + 1) * 512],
                                                        h[a][:, b, t * P:(t + 1) * P],
                                                        wout[w][:, b, half * 512:(half + 1) * 512],
                                                        start=(n == 0), stop=(n == 3 * GB - 1))
                            n += 1
                    last.then_inc(y_ready, 1)

            with pe.Fori(0, NG - 1, 1) as i:
                group(i)
            group(NG - 1)
            if feed:
                feed.turn(pe, lambda c: pe.wait_ge(norm.z, TPC * (c + 1)))

        @block.scalar
        def _(act):
            def split_in(blk, slot):
                act.wait_ge(raw_in, 32 * (blk + 1) if isinstance(blk, int) else blk * 32 + 32)
                nc.scalar.activation(win[slot][0][:], wraw[:], ACT.Copy).then_inc(in_hi, 1)

            split_in(0, 0)

            def group(i, last):
                for b in range(GB):
                    blk = i * GB + b
                    for c in range(NCH):
                        u = i * (GB * NCH) + b * NCH + c
                        s = (b * NCH + c) % 2
                        act.wait_ge(au, u + 1)
                        act.wait_ge(hprod, u + 1)
                        nc.scalar.activation(sa[s][:], pa[s][:, 0:CH], ACT.Silu).then_inc(silu, 1)
                        act.wait_ge(hprod, u + 3)
                        nc.scalar.activation(h[0][:, b, c * CH:(c + 1) * CH], hf[:], ACT.Copy).then_inc(h_hi, 1)
                        if c == 0 and not (last and b == GB - 1):
                            split_in(blk + 1, (b + 1) % 2)
                        if c == 1:
                            act.wait_ge(raw_out, blk * 16 + 16)
                            nc.scalar.activation(wout[0][:, b, :], oraw[:], ACT.Copy).then_inc(out_hi, 1)

            with act.Fori(0, NG - 1, 1) as i:
                group(i, False)
            group(NG - 1, True)
            if feed:
                feed.scale(act)

        @block.vector
        def _(dve):
            dve.sem_inc(hprod, 2)
            dve.sem_inc(y_added, 2)
            dve.sem_inc(out_lo, 1)
            dve.sem_inc(h_lo, 1)

            def split_in(blk, slot):
                dve.wait_ge(in_hi, blk + 1)
                nc.vector.tensor_tensor(win[slot][1][:], wraw[:], win[slot][0][:].bitcast(F32), ALU.subtract).then_inc(in_lo, 1)

            split_in(0, 0)
            dve.wait_ge(y_zero, 1)

            def group(i, last):
                for b in range(GB):
                    blk = i * GB + b
                    for c in range(NCH):
                        u = i * (GB * NCH) + b * NCH + c
                        s = (b * NCH + c) % 2
                        dve.wait_ge(silu, u + 1)
                        dve.wait_ge(h_lo, u + 1)
                        nc.vector.tensor_tensor(hf[:], sa[s][:], pu[s][:, 0:CH], ALU.mult).then_inc(hprod, 1)
                        dve.wait_ge(hprod, u + 3)
                        dve.wait_ge(h_hi, u + 1)
                        nc.vector.tensor_tensor(h[1][:, b, c * CH:(c + 1) * CH], hf[:],
                                                h[0][:, b, c * CH:(c + 1) * CH].bitcast(F32), ALU.subtract).then_inc(h_lo, 1)
                        if c == 0 and not (last and b == GB - 1):
                            split_in(blk + 1, (b + 1) % 2)
                        if c == 1:
                            dve.wait_ge(out_hi, blk + 1)
                            nc.vector.tensor_tensor(wout[1][:, b, :], oraw[:], wout[0][:, b, :].bitcast(F32),
                                                    ALU.subtract).then_inc(out_lo, 1)
                if not last:
                    for t in range(NT):
                        dve.wait_ge(y_ready, i * NT + t + 1)
                        nc.vector.tensor_tensor(Y[:, t, :], Y[:, t, :], py[t % 2][:], ALU.add).then_inc(y_added, 1)

            with dve.Fori(0, NG - 1, 1) as i:
                group(i, False)
            group(NG - 1, True)
            norm.start(dve)
            for t in range(NT + 1):
                if t < NT:
                    dve.wait_ge(y_ready, (NG - 1) * NT + t + 1)
                    nc.vector.tensor_tensor(Y[:, t, :], Y[:, t, :], py[t % 2][:], ALU.add).then_inc(y_added, 1)
                    dve.wait_ge(y_added, (NG - 1) * NT + t + 3)
                    norm.sums(dve, t, Y)
                if t >= 1:
                    norm.unit(dve, t - 1, Y)
            if feed:
                for c in range(NCH):
                    feed.rest(dve, c)

        @block.gpsimd
        def _(gp):
            nc.gpsimd.memset(Y[:], 0.0).then_inc(y_zero, 1)
            norm.pool(gp, Y, lambda g: g.wait_ge(out_lo, NB + 1))


def qkv_phase(nc, K, place, banks):
    NH10 = NH + NKV
    with ExitStack() as ctx:
        sem = lambda n: K.semaphore(f"qkv_{n}")
        W = 256
        pieces = [5 * HGW + m * W for m in range((QW + 2 * KVW) // W)]
        wraw = place("qkv_w_raw", [P, KT, W])
        w = [[place(f"qkv_w_{s}_{x}", [P, KT, W], F32R) for x in ("hi", "lo")] for s in range(2)]
        sq = [place(f"qkv_square_{i}", [P, NH10 * DH]) for i in range(2)]
        ra, rb = place("qkv_rope_a", [P, NH10 * DH]), place("qkv_rope_b", [P, NH10 * DH])
        g = place("qk_norm_rows", [P, 2, DH])
        tab = place("rope_tables", [P, 2, NT, DH])
        ss = place("qkv_square_sums", [P, NT, NH10])
        half = place("qkv_minus_half", [P, NH10])
        raw_in, hi, lo, acc, left = sem("raw"), sem("w_hi"), sem("w_lo"), sem("accumulated"), sem("left_psum")
        consts, squared, summed, rstd, roped, chain, pchain, cached = (
            sem(n) for n in ("consts", "squared", "summed", "rstd", "roped", "chain", "pool_chain", "cache_stored"))
        wv = K.w_mix[0].rearrange("(k p) n -> p k n", p=P)
        block = ctx.enter_context(nc.Block())

        @block.sync
        def _(sp):
            for m, col in enumerate(pieces):
                if m:
                    sp.wait_ge(lo, m)
                sp.dma_start(wraw[:], wv[:, :, col:col + W]).then_inc(raw_in, 16)
                if m == 0:
                    sp.dma_start(g[:, 0, :], K.q_g.broadcast_to([P, DH])).then_inc(consts, 16)
                    sp.dma_start(g[:, 1, :], K.k_g.broadcast_to([P, DH])).then_inc(consts, 16)
                    for i in range(2):
                        sp.dma_start(tab[:, i], K.rope[i].rearrange("(t p) d -> p t d", p=P)).then_inc(consts, 16)
            sp.wait_ge(left, 3 * NT)
            sp.dma_start(K.new_v, K.V[:, CTX_T, :]).then_inc(cached, 16)
            sp.wait_ge(roped, NT)
            sp.dma_start(K.new_k, K.QK[:, CTX_T, QW:]).then_inc(cached, 16)
            sp.wait_ge(cached, 32)

        @block.tensor
        def _(pe):
            for m in range(len(pieces)):
                pe.wait_ge(lo, m + 1)
                for t in range(NT):
                    u = m * NT + t
                    if u >= 4:
                        pe.wait_ge(left, u - 3)
                    n = 0
                    for k in range(KT):
                        for a, x in PASSES:
                            last = nc.tensor.matmul(banks[u % 4][:, 0:W], K.A[a][:, k, t * P:(t + 1) * P],
                                                    w[m % 2][x][:, k, :], start=(n == 0), stop=(n == 3 * KT - 1))
                            n += 1
                    last.then_inc(acc, 1)

        @block.scalar
        def _(act):
            for m in range(len(pieces)):
                act.wait_ge(raw_in, 16 * (m + 1))
                if m >= 2:
                    act.wait_ge(acc, NT * (m - 1))
                nc.scalar.activation(w[m % 2][0][:], wraw[:], ACT.Copy).then_inc(hi, 1)
                if m >= 1:
                    for t in range(NT):
                        u = (m - 1) * NT + t
                        act.wait_ge(acc, u + 1)
                        nc.scalar.copy(K.QK[:, t, (m - 1) * W:m * W], banks[u % 4][:, 0:W]).then_inc(left, 1)
            m = len(pieces) - 1
            for t in range(NT + 1):
                if t < NT:
                    u = m * NT + t
                    act.wait_ge(acc, u + 1)
                    nc.scalar.copy(K.QK[:, t, QW:], banks[u % 4][:, 0:KVW])
                    nc.scalar.copy(K.V[:, t, :], banks[u % 4][:, KVW:W]).then_inc(left, 1)
                    act.wait_ge(left, u + 1)
                    if t >= 2:
                        act.wait_ge(summed, t - 1)
                    nc.scalar.activation(sq[t % 2][:], K.QK[:, t, :], ACT.Square).then_inc(squared, 1)

        @block.gpsimd
        def _(gp):
            link = Chain(gp, pchain)
            link(nc.gpsimd.memset(half[:], -0.5))
            for t in range(NT):
                gp.wait_ge(summed, t + 1)
                link(nc.gpsimd.tensor_scalar(ss[:, t, :], ss[:, t, :], 1.0 / DH, EPS, ALU.mult, ALU.add))
                nc.gpsimd.tensor_tensor(ss[:, t, :], ss[:, t, :], half[:], ALU.pow).then_inc(rstd, 1)

        @block.vector
        def _(dve):
            link = Chain(dve, chain)
            for m in range(len(pieces)):
                dve.wait_ge(hi, m + 1)
                nc.vector.tensor_tensor(w[m % 2][1][:], wraw[:], w[m % 2][0][:].bitcast(F32), ALU.subtract).then_inc(lo, 1)
            dve.wait_ge(consts, 64)

            def normed(t):
                dve.wait_ge(rstd, t + 1)
                x = K.QK[:, t, :].rearrange("p (h d) -> p h d", d=DH)
                link(nc.vector.tensor_tensor(x, x, ss[:, t, :].unsqueeze(2).broadcast_to([P, NH10, DH]), ALU.mult))
                for i, a, b in ((0, 0, NH), (1, NH, NH10)):
                    ins = nc.vector.tensor_tensor(x[:, a:b, :], x[:, a:b, :], g[:, i, :].unsqueeze(1).broadcast_to([P, b - a, DH]), ALU.mult)
                    link(ins)
                cos = tab[:, 0, t, :].unsqueeze(1).broadcast_to([P, NH10, DH])
                A, B = ra[:].rearrange("p (h d) -> p h d", d=DH), rb[:].rearrange("p (h c s e) -> p h c s e", h=NH10, c=2, s=2)
                link(nc.vector.tensor_tensor(A, x, cos, ALU.mult))
                x5 = K.QK[:, t, :].rearrange("p (h c s e) -> p h c s e", h=NH10, c=2, s=2)
                sin = tab[:, 1, t, :].rearrange("p (c s e) -> p c s e", c=2, s=2)
                for s in range(2):
                    link(nc.vector.tensor_tensor(B[:, :, :, s, :], x5[:, :, :, 1 - s, :],
                                                 sin[:, :, s, :].unsqueeze(1).broadcast_to([P, NH10, 2, DH // 4]), ALU.mult))
                nc.vector.tensor_tensor(K.QK[:, t, :], ra[:], rb[:], ALU.add).then_inc(roped, 1)
                dve.wait_ge(roped, t + 1)

            for t in range(NT + 1):
                if t < NT:
                    dve.wait_ge(squared, t + 1)
                    nc.vector.tensor_reduce(ss[:, t, :], sq[t % 2][:].rearrange("p (h d) -> p h d", d=DH), AX_X, ALU.add).then_inc(summed, 1)
                if t >= 1:
                    normed(t - 1)


def attention_phase(nc, K, place, banks):
    HPK = NH // NKV
    with ExitStack() as ctx:
        sem = lambda n: K.semaphore(f"att_{n}")
        NKT = 2 + NT
        LATK = 2 + CTX_T
        SC = DH ** -0.5
        kT = [place(f"kT_{x}", [P, NKT * P], F32R) for x in ("hi", "lo")]
        vs = place("v_hi_lo", [P, NKT, NKV, 2, DH], F32R)
        qs = place("q_stage", [P, HPK, NKV, DH])
        qT = [place(f"qT_{x}", [P, HPK * P], F32R) for x in ("hi", "lo")]
        spare = Plan(nc, K.o_at)
        pr = [[(spare if i == 0 and s < 3 else place)(f"probs_{i}_{s}", [P, LATK * P]) for s in range(HPK)] for i in range(2)]
        assert spare.at <= K.o_at + 4 * HGH * TOK
        pt = [[place(f"probsT_{i}_{x}", [P, HPK * P], F32R) for x in ("hi", "lo")] for i in range(2)]
        ck, cv = place("cache_k_rows", [P, 2, KVW]), place("cache_v_rows", [P, 2, KVW])
        nm = place("neg_max", [P, 2, HPK])
        rsum = place("prob_sums", [P, 2, HPK])
        rinv = place("prob_sum_inverse", [P, HPK])
        rrow = place("inverse_rows", [DH, HPK * P])
        lowh = place("pv_low_half", [DH, HPK * P])
        osum = place("pv_sum", [DH, HPK * P])
        S5 = K.score_banks
        T = [banks[5], banks[6]]
        OB = banks[7]
        cache_in, k_t, k_hi, k_lo, v_hi, v_lo = (sem(n) for n in ("cache_in", "k_turned", "k_hi", "k_lo", "v_hi", "v_lo"))
        q_st, q_t, q_hi, q_lo = (sem(n) for n in ("q_staged", "q_turned", "q_hi", "q_lo"))
        qk, mx, nmx, ex, rc = (sem(n) for n in ("scores", "max", "neg_max", "exp", "inverse"))
        p_t, p_hi, p_lo, pv = (sem(n) for n in ("probs_turned", "probs_hi", "probs_lo", "pv"))
        r_m, r_c, o_low, o_sum, o_out = (sem(n) for n in ("rows_made", "rows_copied", "low_copied", "o_summed", "o_out"))
        block = ctx.enter_context(nc.Block())
        ktile = lambda n: (ck[:, n, :] if n < 2 else K.QK[:, n - 2, QW:])
        kbatches = [list(range(a, min(a + 4, NKT))) for a in range(0, NKT, 4)]

        NU = CTX_T * NKV

        def unit(t, kv):
            if isinstance(t, int) and t == CTX_T:
                return dict(t=t, kv=kv, u=NU + kv, kt=[NKT - 1], b0=NU * LATK + kv)
            u = t * NKV + kv
            return dict(t=t, kv=kv, u=u, kt=list(range(LATK)), b0=u * LATK)

        def cuts(prev):
            n = len(prev["kt"]) if prev else 0
            edges = [-(-n * s // HPK) for s in range(HPK + 1)]
            return [range(edges[s], edges[s + 1]) for s in range(HPK)]

        def run(eng, step):
            step(unit(0, 0), None, None)
            step(unit(0, 1), unit(0, 0), None)
            step(unit(1, 0), unit(0, 1), unit(0, 0))
            with eng.Fori(1, CTX_T - 1, 1) as t:
                step(unit(t, 1), unit(t, 0), unit(t - 1, 1))
                step(unit(t + 1, 0), unit(t, 1), unit(t, 0))
            L = CTX_T - 1
            step(unit(L, 1), unit(L, 0), unit(L - 1, 1))
            step(unit(CTX_T, 0), unit(L, 1), unit(L, 0))
            step(unit(CTX_T, 1), unit(CTX_T, 0), unit(L, 1))
            step(None, unit(CTX_T, 1), unit(CTX_T, 0))
            step(None, None, unit(CTX_T, 1))

        def score_pieces(cur, s):
            if len(cur["kt"]) == 1:
                return [((NKT - 1) * P, P, 1536 * (s % 2))]
            if s % 2 == 0:
                return [(0, 512, 0), (512, 512, 512), (1024, 256, 1024)]
            return [(256, 512, 1536), (768, 512, 2048), (0, 256, 1280)]

        def score_view(cur, s):
            if len(cur["kt"]) == 1:
                return S5[:, 1536 * (s % 2):1536 * (s % 2) + P]
            return S5[:, 1280 * (s % 2):1280 * (s % 2) + LATK * P]

        def needs_queries(cur):
            return cur is not None and cur["kv"] == 0

        @block.sync
        def _(sp):
            sp.dma_start(ck[:], K.cache_k.rearrange("(t p) h d -> p t (h d)", p=P)).then_inc(cache_in, 16)
            sp.dma_start(cv[:], K.cache_v.rearrange("(t p) h d -> p t (h d)", p=P)).then_inc(cache_in, 16)

        @block.tensor
        def _(pe):
            pe.wait_ge(cache_in, 32)
            for n, batch in enumerate(kbatches):
                if n >= 2:
                    pe.wait_ge(k_lo, n - 1)
                for i, kt in enumerate(batch):
                    last = nc.tensor.transpose(T[n % 2][:, i * P:(i + 1) * P], ktile(kt), K.ident[:])
                last.then_inc(k_t, 1)
            pe.wait_ge(k_lo, len(kbatches))
            pe.wait_ge(v_lo, 2)

            def values(prev, n):
                pe.wait_ge(p_lo, prev["b0"] + n + 3)
                if n == 0:
                    pe.wait_ge(o_sum, prev["u"] + 1)
                cnt = len(prev["kt"])
                for x in range(2):
                    last = nc.tensor.matmul(OB, vs[:, prev["kt"][n], prev["kv"]].rearrange("p x d -> p (x d)"), pt[n % 2][x][:],
                                            start=(n == 0 and x == 0), stop=(n == cnt - 1 and x == 1))
                last.then_inc(pv, 1)

            def turn(prev, n):
                if n == 0:
                    pe.wait_ge(ex, (prev["u"] + 1) * HPK + 2)
                    pe.wait_ge(p_lo, prev["b0"] + 2)
                else:
                    pe.wait_ge(p_lo, prev["b0"] + n + 1)
                if n == 1:
                    pe.wait_ge(r_c, prev["u"] + 1)
                for j in range(HPK):
                    last = nc.tensor.transpose(T[n % 2][:, j * P:(j + 1) * P],
                                               pr[prev["kv"]][j][:, n * P:(n + 1) * P], K.ident[:])
                last.then_inc(p_t, 1)
                if n >= 1:
                    values(prev, n - 1)

            def step(cur, prev, fin):
                if needs_queries(cur):
                    pe.wait_ge(q_st, cur["t"] + 1)
                    for j in range(HPK):
                        last = nc.tensor.transpose(T[0][:, j * P:(j + 1) * P], qs[:, j].rearrange("p k d -> p (k d)"), K.ident[:])
                    last.then_inc(q_t, 1)
                    pe.wait_ge(q_lo, cur["t"] + 1)
                for s, blocks in enumerate(cuts(prev)):
                    if cur:
                        a0, a1 = cur["kv"] * DH, (cur["kv"] + 1) * DH
                        for i, (key, width, col) in enumerate(score_pieces(cur, s)):
                            if i == 0:
                                pe.wait_ge(ex, cur["u"] * HPK + s + 1)
                            if i == 2:
                                pe.wait_ge(ex, cur["u"] * HPK + s + 2)
                            for n, (a, b) in enumerate(PASSES):
                                last = nc.tensor.matmul(S5[:, col:col + width], qT[a][a0:a1, s * P:(s + 1) * P],
                                                        kT[b][a0:a1, key:key + width], start=(n == 0), stop=(n == 2))
                        last.then_inc(qk, 1)
                    if prev:
                        for n in blocks:
                            turn(prev, n)
                if prev:
                    values(prev, len(prev["kt"]) - 1)
                    pe.wait_ge(rc, prev["u"] + 1)
                    pe.wait_ge(r_c, prev["u"] + 1)
                    for j in range(HPK):
                        last = nc.tensor.matmul(T[1][0:DH, j * P:(j + 1) * P], rinv[:, j:j + 1].broadcast_to([P, DH]),
                                                K.ident[:], start=True, stop=True)
                    last.then_inc(r_m, 1)

            run(pe, step)

        @block.scalar
        def _(act):
            act.sem_inc(ex, 2)
            act.sem_inc(r_c, 1)
            act.wait_ge(cache_in, 32)
            nc.scalar.activation(vs[:, 0:2, :, 0, :], cv[:].rearrange("p t (h d) -> p t h d", h=NKV), ACT.Copy).then_inc(v_hi, 1)
            nc.scalar.activation(vs[:, 2:NKT, :, 0, :], K.V[:].rearrange("p t (h d) -> p t h d", h=NKV), ACT.Copy).then_inc(v_hi, 1)
            for n, batch in enumerate(kbatches):
                act.wait_ge(k_t, n + 1)
                c0, wd = batch[0] * P, len(batch) * P
                nc.scalar.activation(kT[0][:, c0:c0 + wd], T[n % 2][:, 0:wd], ACT.Copy).then_inc(k_hi, 1)

            def step(cur, prev, fin):
                if needs_queries(cur):
                    act.wait_ge(q_t, cur["t"] + 1)
                    nc.scalar.activation(qT[0][:], T[0], ACT.Copy).then_inc(q_hi, 1)
                for s, blocks in enumerate(cuts(prev)):
                    for n in blocks:
                        act.wait_ge(p_t, prev["b0"] + n + 1)
                        act.wait_ge(pv, prev["b0"] + (n + 1 if len(prev["kt"]) > 1 else 2))
                        nc.scalar.activation(pt[n % 2][0][:], T[n % 2], ACT.Copy).then_inc(p_hi, 1)
                    if cur:
                        act.wait_ge(nmx, cur["u"] * HPK + s + 1)
                        nc.scalar.activation(pr[cur["kv"]][s][:, 0:len(cur["kt"]) * P], score_view(cur, s), ACT.Exp,
                                             bias=nm[:, cur["kv"], s:s + 1], scale=SC,
                                             accum_out=rsum[:, cur["kv"], s:s + 1]).then_inc(ex, 1)
                if prev:
                    act.wait_ge(r_m, prev["u"] + 2)
                    act.wait_ge(o_out, prev["u"] + 1)
                    nc.scalar.copy(rrow[:], T[1][0:DH, :]).then_inc(r_c, 1)
                    act.wait_ge(pv, prev["b0"] + len(prev["kt"]) + 2)
                    nc.scalar.copy(lowh[:], OB[DH:P, :]).then_inc(o_low, 1)

            run(act, step)

        @block.vector
        def _(dve):
            for s, credit in ((p_lo, 2), (pv, 2), (o_sum, 1), (r_m, 1), (o_out, 1)):
                dve.sem_inc(s, credit)
            dve.wait_ge(v_hi, 2)
            nc.vector.tensor_tensor(vs[:, 0:2, :, 1, :], cv[:].rearrange("p t (h d) -> p t h d", h=NKV),
                                    vs[:, 0:2, :, 0, :].bitcast(F32), ALU.subtract).then_inc(v_lo, 1)
            nc.vector.tensor_tensor(vs[:, 2:NKT, :, 1, :], K.V[:].rearrange("p t (h d) -> p t h d", h=NKV),
                                    vs[:, 2:NKT, :, 0, :].bitcast(F32), ALU.subtract).then_inc(v_lo, 1)
            for n, batch in enumerate(kbatches):
                dve.wait_ge(k_hi, n + 1)
                c0, wd = batch[0] * P, len(batch) * P
                nc.vector.tensor_tensor(kT[1][:, c0:c0 + wd], T[n % 2][:, 0:wd], kT[0][:, c0:c0 + wd].bitcast(F32),
                                        ALU.subtract).then_inc(k_lo, 1)

            def stage(t):
                if not (isinstance(t, int) and t == 0):
                    dve.wait_ge(q_t, t)
                q4 = K.QK[:, bass.ds(t, 1), 0:QW].rearrange("p o (k j d) -> p o k j d", k=NKV, j=HPK)
                for kv in range(NKV):
                    ins = nc.vector.tensor_copy(qs[:, :, kv, :], q4[:, 0, kv, :, :])
                ins.then_inc(q_st, 1)

            def step(cur, prev, fin):
                if needs_queries(cur):
                    stage(cur["t"])
                    dve.wait_ge(q_hi, cur["t"] + 1)
                    nc.vector.tensor_tensor(qT[1][:], T[0], qT[0][:].bitcast(F32), ALU.subtract).then_inc(q_lo, 1)
                for s, blocks in enumerate(cuts(prev)):
                    if prev and s == 0:
                        dve.wait_ge(ex, (prev["u"] + 1) * HPK + 2)
                        dve.wait_ge(r_m, prev["u"] + 1)
                        nc.vector.reciprocal(rinv[:], rsum[:, prev["kv"], :]).then_inc(rc, 1)
                    if cur:
                        h = cur["u"] * HPK + s
                        dve.wait_ge(qk, h + 1)
                        m = nm[:, cur["kv"], s:s + 1]
                        nc.vector.reduce_max(m, score_view(cur, s), AX_X).then_inc(mx, 1)
                        dve.wait_ge(mx, h + 1)
                        nc.vector.tensor_scalar(m, m, -SC, None, ALU.mult).then_inc(nmx, 1)
                    if fin and s == 0:
                        dve.wait_ge(o_low, fin["u"] + 1)
                        nc.vector.tensor_tensor(osum[:], OB[0:DH, :], lowh[:], ALU.add).then_inc(o_sum, 1)
                        dve.wait_ge(o_sum, fin["u"] + 2)
                        dve.wait_ge(r_c, fin["u"] + 2)
                        kt0 = HGH + 2 * fin["kv"]
                        for par in range(2):
                            v = lambda x: x[:].rearrange("p (a b q) -> p a b q", b=2, q=P)[:, :, par, :]
                            last = nc.vector.tensor_tensor(K.O[par * DH:(par + 1) * DH, kt0:kt0 + 2, bass.ds(fin["t"] * P, P)],
                                                           v(osum), v(rrow), ALU.mult)
                        last.then_inc(o_out, 1)
                        dve.wait_ge(o_out, fin["u"] + 2)
                    for n in blocks:
                        dve.wait_ge(p_hi, prev["b0"] + n + 1)
                        nc.vector.tensor_tensor(pt[n % 2][1][:], T[n % 2], pt[n % 2][0][:].bitcast(F32),
                                                ALU.subtract).then_inc(p_lo, 1)

            run(dve, step)


def view_chunks(x):
    return x[:].rearrange("p (c s) -> p c s", s=SCAN)


def hgrn_phase(nc, K, place, banks):
    with ExitStack() as ctx:
        sem = lambda n: K.semaphore(f"scan_{n}")
        raw = place("scan_w_raw", [P, KT, P])
        W = [[place(f"scan_w_{s}_{x}", [P, KT, P], F32R) for x in ("hi", "lo")] for s in range(2)]
        q, gate, acc = place("scan_q", [P, TOK]), place("scan_gate", [P, TOK]), place("scan_out", [P, TOK])
        v = place("scan_v", [P, NT, P])
        B = [[place(f"scan_buf_{d}_{i}", [P, TOK]) for i in range(4)] for d in range(2)]
        kb = place("ke_blocks", [P, 4, 4, P])
        S = place("states", [P, NSC, P])
        am = [place(f"weights_{i}", [P, 4 * P]) for i in range(2)]
        reset = place("scan_reset", [P, CH])
        mask = [place(f"mask_{d}", [P, P]) for d in range(2)]
        ones = place("ones", [P, P])
        zero = place("zero_state", [P, P])
        init = [place(f"init_state_{d}", [P, P]) for d in range(2)]
        fin = [place(f"final_state_{d}", [P, P]) for d in range(2)]
        sc = [place(f"chunk_sums_{d}", [P, 3, NSC]) for d in range(2)]
        lb = place("lower_bounds", [P, 3, 2, HGH])
        cur = place("head_cols", [P, 7])
        proj, tr, ub, ab, ob = banks[0:3], banks[3], banks[4:6], banks[6], banks[7]
        (raw_in, w_hi, w_lo, acc_p, left, lbs, ready, head) = (
            sem(n) for n in ("w_loaded", "w_hi", "w_lo", "projected", "left_psum", "lb_ready", "consts_ready", "head_cols_ready"))
        (logf, sums, sums_e, dev, e_dev, factors) = (
            sem(n) for n in ("logf", "sums", "sums_exp", "deviation", "deviation_exp", "factors"))
        (kt_s, kb_s, a_s, am_s, u_s, st_s, o_s, oe_s) = (
            sem(n) for n in ("ke_turned", "ke_blocks", "weights", "weights_masked", "updates", "states", "out", "out_taken"))
        (init_in, fin_s, sq_s, ss_s, ms_s, rs_s, head_end) = (
            sem(n) for n in ("init_loaded", "final_ready", "squares", "square_sums", "mean_squares", "rstd", "head_end"))
        stored, chain, pchain = sem("states_stored"), sem("chain"), sem("pool_chain")
        wv = K.w_mix[0].rearrange("(k p) n -> p k n", p=P)
        COLS = [2 * HGW, 3 * HGW, HGW, 0, 4 * HGW]
        NBLK, NU = len(COLS), 4 * NCH + NT
        rounds = [[[0, 1, 2, 3], [4, 5, 6, 7], [8]], [[7, 6, 5, 4], [3, 2, 1, 0], [8]]]
        out_of = [0, NCH, 2 * NCH, 2 * NCH + NT, 3 * NCH + NT]
        CPT = P // SCAN

        def before(d, c):
            if c == (0, LSC - 1)[d]:
                return init[d][:]
            if c == (LSC, NSC - 1)[d]:
                return zero[:]
            return S[:, c, :]

        def after(d, c):
            if c == (LSC - 1, 0)[d]:
                return None
            if c == (NSC - 1, LSC)[d]:
                return fin[d][:]
            return S[:, c + (1, -1)[d], :]

        block = ctx.enter_context(nc.Block())

        @block.sync
        def _(sp):
            with sp.Fori(1, HGH + 1, 1) as n:
                sp.wait_ge(o_s, n * 6 - 4)
                for d, src in enumerate((K.state_f, K.state_b)):
                    sp.dma_start(init[d][:], src[bass.ds(n - 1, 1)].rearrange("o k v -> (o k) v")).then_inc(init_in, 16)
                for b, col in enumerate(COLS):
                    sp.wait_ge(w_lo, n * NBLK + (b + 1 - NBLK))
                    sp.dma_start(raw[:], wv[:, :, bass.ds(n * P + (col - P), P)]).then_inc(raw_in, 16)
                sp.wait_ge(fin_s, n * 2)
                for d, dst in enumerate((K.new_f, K.new_b)):
                    sp.dma_start(dst[bass.ds(n - 1, 1)].rearrange("o k v -> (o k) v"), fin[d][:]).then_inc(stored, 16)

            sp.wait_ge(stored, HGH * 32 + 32)

        @block.gpsimd
        def _(gp):
            link = Chain(gp, pchain)
            link(nc.gpsimd.memset(kb[:], 0.0))
            link(nc.gpsimd.memset(zero[:], 0.0))
            link(nc.gpsimd.memset(ones[:], 1.0))
            link(nc.gpsimd.memset(reset[:], 1.0))
            link(nc.gpsimd.memset(view_chunks(reset)[:, :, 0:1], 0.0))
            for d in range(2):
                m3 = view_chunks(mask[d])
                link(nc.gpsimd.memset(mask[d][:], 1.0))
                link(nc.gpsimd.affine_select(out=m3, in_=m3, compare_op=ALU.is_ge, fill=0.0, base=0,
                                             pattern=[[-SCAN, CPT], [0, SCAN]], channel_multiplier=1))
                link(nc.gpsimd.affine_select(out=m3, in_=m3, compare_op=ALU.is_ge, fill=0.0, base=SCAN - 1,
                                             pattern=[[SCAN, CPT], [0, SCAN]], channel_multiplier=-1))
                s = (1, -1)[d]
                link(nc.gpsimd.affine_select(out=mask[d][:], in_=mask[d][:], compare_op=ALU.is_ge, fill=0.0, base=0,
                                             pattern=[[s, P]], channel_multiplier=-s))
            gp.sem_inc(ready, 1)

        @block.tensor
        def _(pe):
            pe.wait_ge(ready, 1)

            def project(h):
                pe.wait_ge(ms_s, h * NCH + NCH)
                for b in range(NBLK):
                    slot = b % 2
                    pe.wait_ge(w_lo, h * NBLK + b + 2)
                    for i in range(NT if b == 2 else NCH):
                        u = out_of[b] + i
                        pe.wait_ge(left, h * NU + u + 1)
                        n = 0
                        for k in range(KT):
                            for x, y in PASSES:
                                if b == 2:
                                    last = nc.tensor.matmul(proj[u % 3][:, 0:P], K.A[x][:, k, i * P:(i + 1) * P],
                                                            W[slot][y][:, k, :], start=(n == 0), stop=(n == 3 * KT - 1))
                                else:
                                    last = nc.tensor.matmul(proj[u % 3][:, 0:CH], W[slot][x][:, k, :],
                                                            K.A[y][:, k, i * CH:(i + 1) * CH], start=(n == 0), stop=(n == 3 * KT - 1))
                                n += 1
                        last.then_inc(acc_p, 1)

            def direction(h, d):
                Bk, Bq, Bi, Bd = B[d]
                pe.wait_ge(factors, h * 2 + d + 1)
                for r, tiles in enumerate(rounds[d]):
                    R = h * 6 + 3 * d + r
                    pe.wait_ge(kb_s, R + 1)
                    for j, t in enumerate(tiles):
                        last = nc.tensor.transpose(tr[:, j * P:(j + 1) * P], Bk[:, t * P:(t + 1) * P], K.ident[:])
                    last.then_inc(kt_s, 1)
                    pe.wait_ge(am_s, R + 1)
                    for j, t in enumerate(tiles):
                        last = nc.tensor.matmul(ab[:, j * P:(j + 1) * P], Bd[:, t * P:(t + 1) * P], Bq[:, t * P:(t + 1) * P],
                                                start=True, stop=True)
                    last.then_inc(a_s, 1)
                    pe.wait_ge(kb_s, R + 2)
                    for j, t in enumerate(tiles):
                        p = 9 * d + 4 * r + j
                        pe.wait_ge(st_s, h * 18 + p + 1)
                        for c in range(CPT):
                            last = nc.tensor.matmul(ub[p % 2][:, c * P:(c + 1) * P], kb[:, j, c, :], v[:, t, :],
                                                    start=True, stop=True)
                        last.then_inc(u_s, 1)
                    pe.wait_ge(am_s, R + 2)
                    pe.wait_ge(oe_s, R + 1)
                    for j, t in enumerate(tiles):
                        p = 9 * d + 4 * r + j
                        pe.wait_ge(st_s, h * 18 + p + 3)
                        nc.tensor.matmul(ob[:, j * P:(j + 1) * P], v[:, t, :], am[(3 * d + r) % 2][:, j * P:(j + 1) * P],
                                         start=True, stop=False)
                        for c in range(CPT):
                            a = j * P + c * SCAN
                            last = nc.tensor.matmul(ob[:, a:a + SCAN], before(d, t * CPT + c),
                                                    Bi[:, t * P + c * SCAN:t * P + (c + 1) * SCAN],
                                                    start=False, stop=(c == CPT - 1))
                    last.then_inc(o_s, 1)

            with pe.Fori(0, HGH, 1) as h:
                project(h)
                pe.wait_ge(init_in, h * 32 + 32)
                for d in range(2):
                    direction(h, d)
                pe.wait_ge(sq_s, h + 1)
                for c in range(NCH):
                    nc.tensor.matmul(proj[c][:, 0:CH], ones[:], B[0][1][:, c * CH:(c + 1) * CH],
                                     start=True, stop=True).then_inc(ss_s, 1)

        @block.scalar
        def _(act):
            act.sem_inc(left, 3)
            act.sem_inc(kb_s, 1)
            act.wait_ge(lbs, 1)
            for d in range(2):
                nc.scalar.activation(lb[:, 0, d, :], K.lbd[:, d, :], ACT.Sigmoid)
                last = nc.scalar.activation(lb[:, 1, d, :], K.lbd[:, d, :], ACT.Sigmoid, scale=-1.0)
            last.then_inc(lbs, 1)

            def evacuate(h, b):
                dst = {0: B[0][0], 1: B[1][0], 3: q, 4: gate}.get(b)
                if b == 4:
                    act.wait_ge(head_end, h + 1)
                for i in range(NT if b == 2 else NCH):
                    u = out_of[b] + i
                    act.wait_ge(acc_p, h * NU + u + 1)
                    if b == 2:
                        nc.scalar.copy(v[:, i, :], proj[u % 3][:, 0:P]).then_inc(left, 1)
                    else:
                        nc.scalar.activation(dst[:, i * CH:(i + 1) * CH], proj[u % 3][:, 0:CH],
                                             ACT.Sigmoid if b < 2 else ACT.Silu).then_inc(left, 1)

            def split(h, b):
                act.wait_ge(raw_in, (h * NBLK + b) * 16 + 16)
                if b >= 2:
                    act.wait_ge(acc_p, h * NU + out_of[b - 1])
                nc.scalar.activation(W[b % 2][0][:], raw[:], ACT.Copy).then_inc(w_hi, 1)

            def gates(h, d):
                act.wait_ge(left, h * NU + out_of[d + 1] + 3)
                act.wait_ge(head, h * 2 + 1)
                nc.scalar.activation(B[d][1][:], B[d][0][:], ACT.Ln, bias=cur[:, d:d + 1], scale=cur[:, 2 + d:3 + d]).then_inc(logf, 1)
                act.wait_ge(sums, h * 2 + d + 1)
                nc.scalar.activation(sc[d][:], sc[d][:], ACT.Exp).then_inc(sums_e, 1)
                act.wait_ge(dev, h * 2 + d + 1)
                nc.scalar.activation(B[d][1][:], B[d][2][:], ACT.Exp)
                nc.scalar.activation(B[d][3][:], B[d][2][:], ACT.Exp, scale=-1.0).then_inc(e_dev, 1)

            with act.Fori(0, HGH, 1) as h:
                split(h, 0)
                split(h, 1)
                evacuate(h, 0)
                split(h, 2)
                evacuate(h, 1)
                split(h, 3)
                gates(h, 0)
                evacuate(h, 2)
                split(h, 4)
                gates(h, 1)
                evacuate(h, 3)
                evacuate(h, 4)
                for d in range(2):
                    for r, tiles in enumerate(rounds[d]):
                        R = h * 6 + 3 * d + r
                        act.wait_ge(kt_s, R + 1)
                        act.wait_ge(u_s, h * 18 + 9 * d + 4 * r + 1)
                        for c in range(CPT):
                            rows = slice(c * SCAN, (c + 1) * SCAN)
                            last = nc.scalar.copy(kb[rows, 0:len(tiles), c, :],
                                                  tr[rows, 0:len(tiles) * P].rearrange("p (j k) -> p j k", k=P))
                        last.then_inc(kb_s, 1)
                act.wait_ge(oe_s, h * 6 + 7)
                nc.scalar.activation(B[0][1][:], acc[:], ACT.Square).then_inc(sq_s, 1)
                act.wait_ge(ms_s, h * NCH + 2 * NCH)
                nc.scalar.activation(B[0][3][:], B[0][3][:], ACT.Ln).then_inc(rs_s, 1)
                act.wait_ge(rs_s, h * 2 + 1)
                nc.scalar.activation(B[0][3][:], B[0][3][:], ACT.Exp, scale=-0.5).then_inc(rs_s, 1)

        @block.vector
        def _(dve):
            for s, credit in ((w_lo, 1), (am_s, 1), (st_s, 2), (o_s, 2), (oe_s, 1), (u_s, 1), (ms_s, NCH), (head_end, 1), (stored, 32)):
                dve.sem_inc(s, credit)
            dve.sem_inc(lbs, 1)
            dve.wait_ge(lbs, 2)
            nc.vector.tensor_scalar(lb[:, 2], lb[:, 1], -1.0, None, ALU.mult).then_inc(lbs, 1)
            dve.wait_ge(lbs, 3)
            link = LoopChain(dve, chain)
            rev = lambda x: x[:, ::-1]

            def split(h, b):
                dve.wait_ge(w_hi, h * NBLK + b + 1)
                nc.vector.tensor_tensor(W[b % 2][1][:], raw[:], W[b % 2][0][:].bitcast(F32), ALU.subtract).then_inc(w_lo, 1)

            def columns(h):
                for i in range(3):
                    for d in range(2):
                        link(nc.vector.tensor_copy(cur[:, 2 * i + d:2 * i + d + 1], lb[:, i, d, bass.ds(h, 1)]))
                nc.vector.tensor_copy(cur[:, 6:7], K.cols[:, bass.ds(h + C_HGN, 1)]).then_inc(head, 2)

            def gates(h, d):
                Bk, Bl, Bg, _ = B[d]
                dve.wait_ge(logf, h * 2 + d + 1)
                link(nc.vector.tensor_scalar(Bk[:], Bk[:], cur[:, 4 + d:5 + d], cur[:, 2 + d:3 + d], ALU.mult, ALU.add))
                for c in range(NCH):
                    a = c * CH
                    src, dst = Bl[:, a:a + CH], Bg[:, a:a + CH]
                    if d:
                        src, dst = rev(src), rev(dst)
                    link(nc.vector.tensor_tensor_scan(dst, reset[:], src, 0.0, ALU.mult, ALU.add))
                g3 = view_chunks(Bg)
                mid, end = (SCAN // 2 - 1, SCAN - 1) if d == 0 else (SCAN // 2, 0)
                link(nc.vector.tensor_copy(sc[d][:, 0, :], g3[:, :, mid]))
                link(nc.vector.tensor_copy(sc[d][:, 1, :], g3[:, :, end]))
                link(nc.vector.tensor_tensor(sc[d][:, 2, :], sc[d][:, 1, :], sc[d][:, 0, :], ALU.subtract))
                nc.vector.tensor_tensor(g3, g3, sc[d][:, 0, :].unsqueeze(2).broadcast_to([P, NSC, SCAN]), ALU.subtract).then_inc(dev, 1)
                dve.wait_ge(dev, h * 2 + d + 1)
                dve.sem_inc(sums, 1)

            def products(h, d):
                Bk, Bq, Bi, Bd = B[d]
                dve.wait_ge(sums_e, h * 2 + d + 1)
                dve.wait_ge(e_dev, h * 2 + d + 1)
                dve.wait_ge(left, h * NU + out_of[4] + 3)
                bc = lambda i: sc[d][:, i, :].unsqueeze(2).broadcast_to([P, NSC, SCAN])
                link(nc.vector.tensor_tensor(Bq[:], q[:], Bq[:], ALU.mult))
                link(nc.vector.tensor_tensor(Bd[:], Bk[:], Bd[:], ALU.mult))
                link(nc.vector.tensor_tensor(view_chunks(Bi), view_chunks(Bq), bc(0), ALU.mult))
                nc.vector.tensor_tensor(view_chunks(Bk), view_chunks(Bd), bc(2), ALU.mult).then_inc(factors, 1)

            def take_out(h, d, r):
                tiles = rounds[d][r]
                R = h * 6 + 3 * d + r
                dve.wait_ge(o_s, R + 3)
                if d == 0:
                    lo = tiles[0] * P
                    nc.vector.tensor_copy(acc[:, lo:lo + len(tiles) * P], ob[:, 0:len(tiles) * P]).then_inc(oe_s, 1)
                else:
                    lo = tiles[-1] * P
                    a3 = acc[:, lo:lo + len(tiles) * P].rearrange("p (j k) -> p j k", k=P)[:, ::-1, :]
                    o3 = ob[:, 0:len(tiles) * P].rearrange("p (j k) -> p j k", k=P)
                    nc.vector.tensor_tensor(a3, o3, a3, ALU.add).then_inc(oe_s, 1)
                dve.wait_ge(oe_s, R + 2)

            def direction(h, d):
                if d:
                    dve.wait_ge(o_s, h * 6 + 3 * d + 2)
                dve.wait_ge(stored, h * 32 + 32)
                dve.wait_ge(init_in, h * 32 + 32)
                for r, tiles in enumerate(rounds[d]):
                    R = h * 6 + 3 * d + r
                    dve.wait_ge(a_s, R + 1)
                    dve.wait_ge(o_s, R + 1)
                    n = len(tiles)
                    nc.vector.tensor_tensor(am[(3 * d + r) % 2][:, 0:n * P].rearrange("p (j i) -> p j i", i=P),
                                            ab[:, 0:n * P].rearrange("p (j i) -> p j i", i=P),
                                            mask[d][:].unsqueeze(1).broadcast_to([P, n, P]), ALU.mult).then_inc(am_s, 1)
                    for j, t in enumerate(tiles):
                        p = 9 * d + 4 * r + j
                        dve.wait_ge(u_s, h * 18 + p + 2)
                        order = range(CPT) if d == 0 else range(CPT - 1, -1, -1)
                        for c in order:
                            dst = after(d, t * CPT + c)
                            if dst is not None:
                                ins = nc.vector.scalar_tensor_tensor(dst, before(d, t * CPT + c),
                                                                     sc[d][:, 1, t * CPT + c:t * CPT + c + 1],
                                                                     ub[p % 2][:, c * P:(c + 1) * P], ALU.mult, ALU.add)
                                link(ins)
                        dve.sem_inc(st_s, 1)
                    if r:
                        take_out(h, d, r - 1)
                take_out(h, d, 2)
                dve.sem_inc(fin_s, 1)

            with dve.Fori(0, HGH, 1) as h:
                link.begin(h, K.scan_links)
                split(h, 0)
                split(h, 1)
                columns(h)
                split(h, 2)
                split(h, 3)
                gates(h, 0)
                split(h, 4)
                gates(h, 1)
                for d in range(2):
                    products(h, d)
                for d in range(2):
                    direction(h, d)
                for c in range(NCH):
                    dve.wait_ge(ss_s, h * NCH + c + 1)
                    nc.vector.tensor_scalar(B[0][3][:, c * CH:(c + 1) * CH], proj[c][:, 0:CH], 1.0 / P, EPS,
                                            ALU.mult, ALU.add).then_inc(ms_s, 1)
                dve.wait_ge(rs_s, h * 2 + 2)
                link(nc.vector.scalar_tensor_tensor(acc[:], acc[:], cur[:, 6:7], B[0][3][:], ALU.mult, ALU.mult))
                nc.vector.tensor_tensor(K.O[:, bass.ds(h, 1), :].rearrange("p o t -> p (o t)"), acc[:], gate[:], ALU.mult).then_inc(head_end, 1)
                dve.wait_ge(head_end, h + 2)
                link.end()


def mix_out_phase(nc, K, place, banks):
    with ExitStack() as ctx:
        sem = lambda n: K.semaphore(f"mixout_{n}")
        Y = K.Y
        wo = [place(f"mixout_w_{x}", [P, KT, D], F32R) for x in ("hi", "lo")]
        raw = [place(f"mixout_w_raw_{i}", [P, D]) for i in range(2)]
        tmp = [place(f"mixout_tmp_{i}", [P, CH]) for i in range(2)]
        gB, bB, xo = (place(f"mixout_{n}", [P, D]) for n in ("ln_g_rows", "ln_b_rows", "x_row"))
        norm = Norm(K, ctx, nc, "mixout", place, 1, 5, K.x1_rows, K.x2_rows, gB[:], bB[:], xo[:])
        feed = Feed(K, ctx, nc, "mixout", Y, tmp, banks[0:4], 7, 6)
        py = K.wide[2:4]
        raw_in = [sem("w_loaded_even"), sem("w_loaded_odd")]
        w_hi, w_lo, o_hi, o_lo, y_ready, y_taken = (sem(n) for n in ("w_hi", "w_lo", "o_hi", "o_lo", "y_ready", "y_taken"))
        wv = K.w_mix_out[0].rearrange("(k p) n -> p k n", p=P)
        block = ctx.enter_context(nc.Block())

        @block.sync
        def _(sp):
            for k in range(KT):
                if k >= 2:
                    sp.wait_ge(w_lo, k - 1)
                sp.dma_start(raw[k % 2][:], wv[:, k, :]).then_inc(raw_in[k % 2], 16)
            norm.load(sp, lambda: None)

        @block.tensor
        def _(pe):
            pe.wait_ge(o_lo, KT)
            for t in range(NT):
                if t >= 2:
                    pe.wait_ge(y_taken, t - 1)
                n = 0
                for k in range(KT):
                    if t == 0:
                        pe.wait_ge(w_lo, k + 1)
                    for a, w in PASSES:
                        for half in range(2):
                            last = nc.tensor.matmul(py[t % 2][:, half * 512:(half + 1) * 512],
                                                    K.A[a][:, k, t * P:(t + 1) * P], wo[w][:, k, half * 512:(half + 1) * 512],
                                                    start=(n == 0), stop=(n == 3 * KT - 1))
                        n += 1
                last.then_inc(y_ready, 1)
            feed.turn(pe, lambda c: pe.wait_ge(norm.z, TPC * (c + 1)))

        @block.scalar
        def _(act):
            for k in range(KT):
                nc.scalar.activation(K.A[0][:, k, :], K.O[:, k, :], ACT.Copy).then_inc(o_hi, 1)
                act.wait_ge(raw_in[k % 2], 16 * (k // 2 + 1))
                nc.scalar.activation(wo[0][:, k, :], raw[k % 2][:], ACT.Copy).then_inc(w_hi, 1)
            feed.scale(act)

        @block.vector
        def _(dve):
            for k in range(KT):
                dve.wait_ge(o_hi, k + 1)
                nc.vector.tensor_tensor(K.A[1][:, k, :], K.O[:, k, :], K.A[0][:, k, :].bitcast(F32), ALU.subtract).then_inc(o_lo, 1)
                dve.wait_ge(w_hi, k + 1)
                nc.vector.tensor_tensor(wo[1][:, k, :], raw[k % 2][:], wo[0][:, k, :].bitcast(F32), ALU.subtract).then_inc(w_lo, 1)
            norm.start(dve)
            dve.wait_ge(o_lo, KT)
            for t in range(NT + 1):
                if t < NT:
                    dve.wait_ge(y_ready, t + 1)
                    norm.sums(dve, t, Y, src=py[t % 2], freed=y_taken)
                if t >= 1:
                    norm.unit(dve, t - 1, Y)
            for c in range(NCH):
                feed.rest(dve, c)

        @block.gpsimd
        def _(gp):
            norm.pool(gp, Y)


def rope_tables(np):
    half = DH // 2
    inv = 10000.0 ** (-np.arange(0, half, 2, dtype=np.float32) / half)
    n = np.arange(N_LAT)
    row = (n // GRID_W).astype(np.float32)[:, None] * inv
    col = (n % GRID_W).astype(np.float32)[:, None] * inv
    cos = np.concatenate([np.cos(row), np.cos(row), np.cos(col), np.cos(col)], 1)
    sin = np.concatenate([-np.sin(row), np.sin(row), -np.sin(col), np.sin(col)], 1)
    tab = np.stack([np.concatenate([cos, np.ones((N_CTX, DH))]), np.concatenate([sin, np.zeros((N_CTX, DH))])])
    return tab.astype(np.float32)


class Kernel:

    def semaphore(self, name):
        self.held.append(self.nc.alloc_semaphore(name))
        return self.held[-1]

    def clear_semaphores(self):
        self.nc.clear_and_free_semaphores(self.held)
        self.nc.all_engine_barrier()
        self.held = []


def program(nc, K):
    K.nc, K.held = nc, []
    place = Plan(nc, (nc.sbuf_base + 63) // 64 * 64)
    K.ident = place("ident", [P, P])
    K.mod = place("mod_cols", [P, 72, 2])
    K.cols = place("param_cols", [P, C_END])
    K.lbd = place("lb_logit_difference", [P, 2, HGH])
    K.A = [place("act_hi", [P, KT, TOK], F32R), place("act_lo", [P, KT, TOK], F32R)]
    K.o_at = place.at
    K.Y = place("Y", [P, NT, D])
    phase = place.at
    mix = Plan(nc, K.o_at)
    K.O = mix("mix_out_T", [P, KT, TOK])
    mix_at = mix.at
    K.QK = mix("qk_rows", [P, NT, QW + KVW])
    K.V = mix("v_rows", [P, NT, KVW])
    att_at = mix.at
    K.scan_links = 97
    with ExitStack() as ctx:
        psum = ctx.enter_context(nc.psum_tensor("psum", [P, 4096], F32))
        K.score_banks = psum[:, 0:2560]
        K.wide = [psum[:, 1024 * i:1024 * (i + 1)] for i in range(4)]
        banks = [psum[:, 512 * i:512 * (i + 1)] for i in range(8)]
        K.mod_rows = nc.dram_tensor("mod_rows", (2, N_MOD * D), F32).ap()
        x1 = nc.dram_tensor("x_after_1", (TOK, D), F32).ap()
        x2 = nc.dram_tensor("x_after_2", (TOK, D), F32).ap()
        K.x_rows = lambda t: K.x_sample[0, t * P:(t + 1) * P, :] if t < CTX_T else K.x_prompt[0]
        K.x1_rows = lambda t: x1[t * P:(t + 1) * P, :]
        K.x2_rows = lambda t: x2[t * P:(t + 1) * P, :]
        y_rows = lambda t: K.y_sample[0, t * P:(t + 1) * P, :] if t < CTX_T else K.y_prompt[0]
        modulation_phase(nc, K, Plan(nc, phase), banks)
        ffn_phase(nc, K, Plan(nc, phase), banks, "ffn1", K.w1_in, K.w1_out, K.x_rows, K.x1_rows, 2, 0, (4, 3))
        qkv_phase(nc, K, Plan(nc, att_at), banks)
        attention_phase(nc, K, Plan(nc, att_at), banks)
        K.clear_semaphores()
        hgrn_phase(nc, K, Plan(nc, mix_at), banks)
        mix_out_phase(nc, K, Plan(nc, phase), banks)
        ffn_phase(nc, K, Plan(nc, phase), banks, "ffn2", K.w2_in, K.w2_out, K.x2_rows, y_rows, 8, 2, None)


_INS = {"x_prompt": "x_prompt", "x_sample": "x_sample", "cache_k": "cache_k", "cache_v": "cache_v",
        "state_f": "state_hgrn_fwd", "state_b": "state_hgrn_bwd", "c": "c", "c_ctx": "c_ctx",
        "w_mod": "w_mod", "b_mod": "b_mod", "w1_in": "w_ffn1_in", "w1_out": "w_ffn1_out",
        "w2_in": "w_ffn2_in", "w2_out": "w_ffn2_out", "w_mix": "w_in", "w_mix_out": "w_out",
        "q_g": "q_norm_g", "k_g": "k_norm_g", "hg_g": "hg_norm_g", "lb_f": "lb_logits_fwd",
        "lb_b": "lb_logits_bwd", "ln_g": "ln_g", "ln_b": "ln_b"}
_OUTS = {"y_prompt": (1, N_CTX, D), "y_sample": (1, N_LAT, D), "new_k": (1, 1, N_CTX, NKV, DH),
         "new_v": (1, 1, N_CTX, NKV, DH), "new_f": (1, 1, HGH, P, P), "new_b": (1, 1, HGH, P, P)}


def kernel(**inputs):
    import numpy as np
    import concourse.bacc as bacc
    from concourse.bass_utils import run_bass_kernel_spmd as run
    nc = bacc.Bacc("TRN2", target_bir_lowering=False, num_devices=1, dynamic_dma_scratch_size=1024)
    K, arrays = Kernel(), {}

    def declare(attr, array):
        arrays["in_" + attr] = np.ascontiguousarray(array)
        K.__dict__[attr] = nc.dram_tensor("in_" + attr, arrays["in_" + attr].shape, F32, kind="ExternalInput").ap()

    for attr, name in _INS.items():
        declare(attr, inputs[name])
    declare("rope", rope_tables(np))
    for name, shape in _OUTS.items():
        K.__dict__[name] = nc.dram_tensor("out_" + name, shape, F32, kind="ExternalOutput").ap()
    K.ln_g, K.ln_b = K.ln_g[0], K.ln_b[0]
    K.cache_k, K.cache_v = K.cache_k[0, 0], K.cache_v[0, 0]
    K.state_f, K.state_b = K.state_f[0, 0], K.state_b[0, 0]
    K.new_f, K.new_b = K.new_f[0, 0], K.new_b[0, 0]
    K.new_k = K.new_k[0, 0].rearrange("t h d -> t (h d)")
    K.new_v = K.new_v[0, 0].rearrange("t h d -> t (h d)")
    program(nc, K)
    r = run(nc, [arrays], core_ids=[0])
    return tuple(r.results[0]["out_" + name] for name in _OUTS)
```

```python
from contextlib import ExitStack

import numpy as np
import concourse.bass as bass
from concourse import mybir

ALU = mybir.AluOpType
ACT = mybir.ActivationFunctionType
F32 = mybir.dt.float32
F32R = mybir.dt.float32r
AX_X = mybir.AxisListType.X

P = 128
D = 1024
KT = D // P
N_LAT, N_CTX = 1024, 128
TOK = N_LAT + N_CTX
NT = TOK // P
CTX_T = N_LAT // P
CH = 384
NCH = TOK // CH
TPC = CH // P
FF = 2816
NB = FF // P
GB = 2
NG = NB // GB
HGW = 512
HGH = 4
NH, NKV, DH = 8, 2, 64
QW, KVW = NH * DH, NKV * DH
IN_W = 5 * HGW + QW + 2 * KVW
PAST = 256
GRID_W = 64
N_MOD = 9
ALPHA = 2.0 ** 0.25
EPS = 1e-6
SCAN = 32
NSC = TOK // SCAN
LSC = N_LAT // SCAN

C_BMOD, C_LNG, C_LNB, C_C, C_CCTX, C_LBF, C_LBB, C_HGN, C_END = 0, 72, 96, 120, 128, 136, 144, 152, 156
PASSES = ((0, 0), (0, 1), (1, 0))


class Plan:

    def __init__(self, nc, base):
        self.nc, self.at = nc, base

    def __call__(self, name, shape, dt=F32):
        size = int(np.prod(shape[1:])) * 4
        t = self.nc.alloc_sbuf_tensor_at(name, shape, dt, offset=self.at)
        self.at += (size + 31) // 32 * 32
        assert self.at <= self.nc.sbuf_usable_end, (name, self.at, self.nc.sbuf_usable_end)
        return t


class Chain:

    def __init__(self, eng, sem):
        self.eng, self.sem, self.n = eng, sem, 0

    def __call__(self, ins):
        self.n += 1
        ins.then_inc(self.sem, 1)
        self.eng.wait_ge(self.sem, self.n)


class LoopChain(Chain):

    def begin(self, i, per, before=0):
        self.per, self.n, self.base = per, 0, i * per + before

    def __call__(self, ins):
        self.n += 1
        ins.then_inc(self.sem, 1)
        self.eng.wait_ge(self.sem, self.base + self.n)

    def end(self):
        assert self.n == self.per, self.n


class Feed:

    def __init__(self, K, ctx, nc, tag, src, tmp, banks, scale_i, shift_i):
        self.K, self.nc, self.src, self.tmp, self.banks = K, nc, src, tmp, banks
        self.scale_i, self.shift_i = scale_i, shift_i
        sem = lambda n: K.semaphore(f"{tag}_{n}")
        self.turned, self.affine, self.hi, self.lo = sem("turned"), sem("affine"), sem("feed_hi"), sem("feed_lo")

    def turn(self, pe, wait_chunk):
        for c in range(NCH):
            wait_chunk(c)
            for k in range(KT):
                n = c * KT + k
                if n >= 4:
                    pe.wait_ge(self.affine, n - 3)
                for j in range(TPC):
                    t = c * TPC + j
                    last = self.nc.tensor.transpose(self.banks[n % 4][:, j * P:(j + 1) * P],
                                                    self.src[:, t, k * P:(k + 1) * P], self.K.ident[:])
                last.then_inc(self.turned, 1)

    def scale(self, act):
        K, nc = self.K, self.nc
        for c in range(NCH):
            for k in range(KT):
                n = c * KT + k
                act.wait_ge(self.turned, n + 1)
                if n >= 2:
                    act.wait_ge(self.lo, n - 1)
                cuts = [(0, CH, 0)] if c < NCH - 1 else [(0, CH - P, 0), (CH - P, CH, 1)]
                for a, b, v in cuts:
                    last = nc.scalar.activation(self.tmp[n % 2][:, a:b], self.banks[n % 4][:, a:b], ACT.Identity,
                                                bias=K.mod[:, self.shift_i * KT + k, v:v + 1],
                                                scale=K.mod[:, self.scale_i * KT + k, v:v + 1])
                last.then_inc(self.affine, 1)
                act.wait_ge(self.affine, n + 1)
                nc.scalar.activation(K.A[0][:, k, c * CH:(c + 1) * CH], self.tmp[n % 2][:], ACT.Copy).then_inc(self.hi, 1)

    def rest(self, dve, c):
        K, nc = self.K, self.nc
        for k in range(KT):
            n = c * KT + k
            dve.wait_ge(self.hi, n + 1)
            nc.vector.tensor_tensor(K.A[1][:, k, c * CH:(c + 1) * CH], self.tmp[n % 2][:],
                                    K.A[0][:, k, c * CH:(c + 1) * CH].bitcast(F32), ALU.subtract).then_inc(self.lo, 1)


class Norm:

    def __init__(self, K, ctx, nc, tag, place, ln_i, gate_i, res_src, out_dst, gB, bB, xo):
        self.K, self.nc, self.ln_i, self.gate_i = K, nc, ln_i, gate_i
        self.res_src, self.out_dst, self.gB, self.bB, self.xo = res_src, out_dst, gB, bB, xo
        sem = lambda n: K.semaphore(f"{tag}_{n}")
        self.gate = place(f"{tag}_gate_rows", [P, 2, D])
        self.xs = place(f"{tag}_residual", [P, D])
        self.st = place(f"{tag}_stats", [P, 2, 6])
        self.mv = place(f"{tag}_meanvar", [P, NT, 2])
        self.rs = place(f"{tag}_rstd", [P, NT])
        self.half = place(f"{tag}_minus_half", [P, 1])
        self.gates, self.rows = sem("gate_rows_loaded"), sem("ln_rows_loaded")
        self.res, self.res_used = sem("residual_loaded"), sem("residual_used")
        self.chain, self.bn, self.rstd, self.z = sem("norm_chain"), sem("bn_done"), sem("rstd_done"), sem("z_done")
        self.pool_chain, self.xo_done, self.stored = sem("pool_chain"), sem("xo_done"), sem("x_stored")

    def load(self, sp, affine_free):
        K = self.K
        for v in range(2):
            sp.dma_start(self.gate[:, v, :], K.mod_rows[v:v + 1, self.gate_i * D:(self.gate_i + 1) * D]
                         .broadcast_to([P, D])).then_inc(self.gates, 16)
        sp.dma_start(self.xs[:], self.res_src(0)).then_inc(self.res, 16)
        affine_free()
        sp.dma_start(self.gB, K.ln_g[self.ln_i:self.ln_i + 1, :].broadcast_to([P, D])).then_inc(self.rows, 16)
        sp.dma_start(self.bB, K.ln_b[self.ln_i:self.ln_i + 1, :].broadcast_to([P, D])).then_inc(self.rows, 16)
        for t in range(1, NT + 2):
            if t < NT:
                sp.wait_ge(self.res_used, t)
                sp.dma_start(self.xs[:], self.res_src(t)).then_inc(self.res, 16)
            if t >= 2:
                sp.wait_ge(self.xo_done, t - 1)
                sp.dma_start(self.out_dst(t - 2), self.xo).then_inc(self.stored, 16)
        sp.wait_ge(self.stored, 16 * NT)

    def start(self, dve):
        self.link = Chain(dve, self.chain)

    def sums(self, dve, t, Y, src=None, freed=None):
        nc, v = self.nc, int(t == CTX_T)
        if t == 0:
            dve.wait_ge(self.gates, 32)
        ins = nc.vector.tensor_tensor(Y[:, t, :], Y[:, t, :] if src is None else src, self.gate[:, v, :], ALU.mult)
        if freed is not None:
            ins.then_inc(freed, 1)
            dve.wait_ge(freed, t + 1)
        else:
            self.link(ins)
        dve.wait_ge(self.res, 16 * (t + 1))
        nc.vector.scalar_tensor_tensor(Y[:, t, :], self.xs[:], ALPHA, Y[:, t, :], ALU.mult, ALU.add).then_inc(self.res_used, 1)
        dve.wait_ge(self.res_used, t + 1)
        if t:
            dve.wait_ge(self.bn, t)
        for h in range(2):
            self.link(nc.vector.bn_stats(self.st[:, h, :], Y[:, t, h * 512:(h + 1) * 512]))
        nc.vector.bn_aggr(self.mv[:, t, :], self.st[:]).then_inc(self.bn, 1)

    def unit(self, dve, t, Y):
        dve.wait_ge(self.bn, t + 1)
        dve.wait_ge(self.rstd, t + 1)
        self.nc.vector.tensor_scalar(Y[:, t, :], Y[:, t, :], self.mv[:, t, 0:1], self.rs[:, t:t + 1],
                                     ALU.subtract, ALU.mult).then_inc(self.z, 1)

    def pool(self, gp, Y, xo_free=None):
        nc = self.nc
        link = Chain(gp, self.pool_chain)
        link(nc.gpsimd.memset(self.half[:], -0.5))

        def rstd(t):
            gp.wait_ge(self.bn, t + 1)
            link(nc.gpsimd.tensor_scalar(self.rs[:, t:t + 1], self.mv[:, t, 1:2], EPS, None, ALU.add))
            nc.gpsimd.tensor_tensor(self.rs[:, t:t + 1], self.rs[:, t:t + 1], self.half[:], ALU.pow).then_inc(self.rstd, 1)

        rstd(0)
        for t in range(NT):
            if t + 1 < NT:
                rstd(t + 1)
            if t == 0:
                gp.wait_ge(self.rows, 32)
                if xo_free is not None:
                    xo_free(gp)
            else:
                gp.wait_ge(self.stored, 16 * t)
            gp.wait_ge(self.z, t + 1)
            link(nc.gpsimd.tensor_tensor(self.xo, Y[:, t, :], self.gB, ALU.mult))
            nc.gpsimd.tensor_tensor(self.xo, self.xo, self.bB, ALU.add).then_inc(self.xo_done, 1)


def modulation_phase(nc, K, place, banks):
    with ExitStack() as ctx:
        sem = lambda n: K.semaphore(f"mod_{n}")
        rows1 = place("param_rows_1", [P, P])
        rows2 = place("param_rows_2", [C_END - P, P])
        silu = place("silu_cond", [P, KT, 2])
        wbuf = [place(f"w_mod_{i}", [P, KT, D]) for i in range(2)]
        tmp = [place(f"mod_tmp_{i}", [P, CH]) for i in range(2)]
        bounce = place("mod_bounce", [P, 2, P])
        ncol = place("mod_scratch", [P, 16, 2])
        feed = Feed(K, ctx, nc, "mod", K.Y, tmp, [banks[i] for i in range(4)], 1, 0)
        p_col, p_mod = banks[4], banks[5]
        rows_in, ident_ok, cols_t, cols_ok, silu_ok = (sem(n) for n in ("rows_in", "ident_ok", "cols_turned", "cols_ok", "silu_ok"))
        w_in = [sem("w_in_even"), sem("w_in_odd")]
        w_used, chain, mod_ok = (sem(n) for n in ("w_used", "chain", "mod_ok"))
        x_in, pool_chain, r_turned, r_ok, r_out = (sem(n) for n in ("x_in", "pool_chain", "rows_turned", "rows_ok", "rows_out"))
        w_mod = K.w_mod[0].rearrange("(k p) n -> p k n", p=P)
        block = ctx.enter_context(nc.Block())

        @block.sync
        def _(sp):
            vec = lambda a, n: a.rearrange("(j p) -> j p", p=P) if n else a
            sp.dma_start(rows1[C_BMOD:C_LNG, :], K.b_mod[0].rearrange("(j p) -> j p", p=P)).then_inc(rows_in, 16)
            sp.dma_start(rows1[C_LNG:C_LNB, :], K.ln_g.rearrange("l (j p) -> (l j) p", p=P)).then_inc(rows_in, 16)
            sp.dma_start(rows1[C_LNB:C_C, :], K.ln_b.rearrange("l (j p) -> (l j) p", p=P)).then_inc(rows_in, 16)
            sp.dma_start(rows1[C_C:C_CCTX, :], K.c[0].rearrange("(j p) -> j p", p=P)).then_inc(rows_in, 16)
            sp.dma_start(rows2[0:C_LBF - P, :], K.c_ctx.rearrange("(j p) -> j p", p=P)).then_inc(rows_in, 16)
            sp.dma_start(rows2[C_LBF - P:C_LBB - P, :], K.lb_f.rearrange("l (j p) -> (l j) p", p=P)).then_inc(rows_in, 16)
            sp.dma_start(rows2[C_LBB - P:C_HGN - P, :], K.lb_b.rearrange("l (j p) -> (l j) p", p=P)).then_inc(rows_in, 16)
            sp.dma_start(rows2[C_HGN - P:C_END - P, :], K.hg_g[0].rearrange("(j p) -> j p", p=P)).then_inc(rows_in, 16)
            for m in range(N_MOD):
                if m >= 2:
                    sp.wait_ge(w_used, m - 1)
                sp.dma_start(wbuf[m % 2][:], w_mod[:, :, m * D:(m + 1) * D]).then_inc(w_in[m % 2], 16)
                if m == 1:
                    for t in range(NT):
                        sp.dma_start(K.Y[:, t, :], K.x_rows(t)).then_inc(x_in, 16)
            for v in range(2):
                sp.wait_ge(r_ok, v + 1)
                sp.dma_start(K.mod_rows[v].rearrange("(j p) -> j p", p=P), bounce[0:72, v, :]).then_inc(r_out, 16)
            sp.wait_ge(r_out, 32)

        @block.gpsimd
        def _(gp):
            link = Chain(gp, pool_chain)
            link(nc.gpsimd.memset(K.ident[:], 0.0))
            nc.gpsimd.affine_select(out=K.ident[:], in_=K.ident[:], compare_op=ALU.not_equal, fill=1.0, base=0,
                                    pattern=[[-1, P]], channel_multiplier=1).then_inc(ident_ok, 1)

        @block.tensor
        def _(pe):
            pe.wait_ge(ident_ok, 1)
            pe.wait_ge(rows_in, 128)
            nc.tensor.transpose(p_col[:, 0:P], rows1[:], K.ident[:])
            nc.tensor.transpose(p_col[:, P:C_END], rows2[:], K.ident[0:C_END - P, 0:C_END - P]).then_inc(cols_t, 1)
            pe.wait_ge(silu_ok, 1)
            for m in range(N_MOD):
                pe.wait_ge(w_in[m % 2], 16 * (m // 2 + 1))
                for j in range(KT):
                    col = 2 * (m * KT + j)
                    for k in range(KT):
                        last = nc.tensor.matmul(p_mod[:, col:col + 2], wbuf[m % 2][:, k, j * P:(j + 1) * P],
                                                silu[:, k, :], start=(k == 0), stop=(k == KT - 1))
                last.then_inc(w_used, 1)
            pe.wait_ge(mod_ok, 1)
            for v in range(2):
                nc.tensor.transpose(p_col[0:72, v * P:(v + 1) * P], K.mod[:, :, v], K.ident[:]).then_inc(r_turned, 1)
            feed.turn(pe, lambda c: pe.wait_ge(x_in, 16 * NT) if c == 0 else None)

        @block.scalar
        def _(act):
            act.wait_ge(cols_ok, 1)
            nc.scalar.activation(silu[:].rearrange("p k v -> p v k"),
                                 K.cols[:, C_C:C_LBF].rearrange("p (v k) -> p v k", v=2), ACT.Silu).then_inc(silu_ok, 1)
            act.wait_ge(mod_ok, 1)
            for v in range(2):
                act.wait_ge(r_turned, 2)
                nc.scalar.copy(bounce[0:72, v, :], p_col[0:72, v * P:(v + 1) * P]).then_inc(r_ok, 1)
            feed.scale(act)

        @block.vector
        def _(dve):
            link = Chain(dve, chain)
            dve.wait_ge(cols_t, 1)
            nc.vector.tensor_copy(K.cols[:], p_col[:, 0:C_END]).then_inc(cols_ok, 1)
            dve.wait_ge(cols_ok, 1)
            for i, c0 in enumerate((C_LBF, C_LBB)):
                link(nc.vector.tensor_tensor(K.lbd[:, i, :], K.cols[:, c0:c0 + HGH], K.cols[:, c0 + HGH:c0 + 2 * HGH], ALU.subtract))
            dve.wait_ge(w_used, N_MOD)
            M = K.mod
            link(nc.vector.tensor_tensor(M[:], p_mod[:, 0:144].rearrange("p (j v) -> p j v", v=2),
                                         K.cols[:, 0:72].unsqueeze(2).broadcast_to([P, 72, 2]), ALU.add))
            grp = lambda i: M[:, i * KT:(i + 1) * KT, :]
            for i in (1, 4, 7):
                link(nc.vector.tensor_scalar(grp(i), grp(i), 1.0, None, ALU.add))
            for i in (2, 8):
                link(nc.vector.tensor_scalar(grp(i), grp(i), 0.5, None, ALU.mult))
            for l, (ish, isc) in enumerate(((3, 4), (6, 7))):
                g = K.cols[:, C_LNG + l * KT:C_LNG + (l + 1) * KT].unsqueeze(2).broadcast_to([P, KT, 2])
                b = K.cols[:, C_LNB + l * KT:C_LNB + (l + 1) * KT].unsqueeze(2).broadcast_to([P, KT, 2])
                link(nc.vector.tensor_tensor(ncol[:, 0:KT, :], grp(isc), b, ALU.mult))
                link(nc.vector.tensor_tensor(grp(ish), grp(ish), ncol[:, 0:KT, :], ALU.add))
                link(nc.vector.tensor_tensor(grp(isc), grp(isc), g, ALU.mult))
            nc.vector.memset(ncol[:, 0:1, 0:1], 0.0).then_inc(mod_ok, 1)
            for c in range(NCH):
                feed.rest(dve, c)


def ffn_phase(nc, K, place, banks, tag, w_in, w_out, res_src, out_dst, gate_i, ln_i, feed_i):
    with ExitStack() as ctx:
        sem = lambda n: K.semaphore(f"{tag}_{n}")
        Y = K.Y
        win = [[place(f"{tag}_win_{s}_{x}", [P, 2, KT, P], F32R) for x in ("hi", "lo")] for s in range(2)]
        raw_at = place.at
        wraw = place(f"{tag}_win_raw", [P, 2, KT, P])
        gB = nc.alloc_sbuf_tensor_at(f"{tag}_ln_g_rows", [P, D], F32, offset=raw_at)
        bB = nc.alloc_sbuf_tensor_at(f"{tag}_ln_b_rows", [P, D], F32, offset=raw_at + 4 * D)
        wout = [place(f"{tag}_wout_{x}", [P, GB, D], F32R) for x in ("hi", "lo")]
        out_at = place.at
        oraw = place(f"{tag}_wout_raw", [P, D])
        xo = nc.alloc_sbuf_tensor_at(f"{tag}_x_row", [P, D], F32, offset=out_at)
        h = [place(f"{tag}_h_{x}", [P, GB, TOK], F32R) for x in ("hi", "lo")]
        sa = [place(f"{tag}_silu_{i}", [P, CH]) for i in range(2)]
        hf = place(f"{tag}_h", [P, CH])
        norm = Norm(K, ctx, nc, tag, place, ln_i, gate_i, res_src, out_dst, gB[:], bB[:], xo[:])
        feed = None
        if feed_i is not None:
            feed = Feed(K, ctx, nc, tag, Y, sa, banks[0:4], *feed_i)
        pa, pu = banks[0:2], banks[2:4]
        py = K.wide[2:4]
        raw_in, in_hi, in_lo = sem("win_loaded"), sem("win_hi"), sem("win_lo")
        raw_out, out_hi, out_lo = sem("wout_loaded"), sem("wout_hi"), sem("wout_lo")
        au, silu, hprod, h_hi, h_lo = sem("au_ready"), sem("silu_done"), sem("h_done"), sem("h_hi"), sem("h_lo")
        y_ready, y_added, y_zero = sem("y_ready"), sem("y_added"), sem("y_zeroed")
        wi_v = w_in[0].rearrange("(k p) (s n) -> p s k n", p=P, s=2)
        wo_v = w_out[0].rearrange("(b p) n -> p b n", p=P)
        block = ctx.enter_context(nc.Block())

        @block.sync
        def _(sp):
            def load_in(blk):
                for s in range(2):
                    sp.dma_start(wraw[:, s], wi_v[:, s, :, bass.ds(blk * P, P)]).then_inc(raw_in, 16)

            load_in(0)

            def group(i, last):
                for b in range(GB):
                    blk = i * GB + b
                    if not (last and b == GB - 1):
                        sp.wait_ge(in_lo, blk + 1)
                        load_in(blk + 1)
                    sp.wait_ge(out_lo, blk + 1)
                    sp.dma_start(oraw[:], wo_v[:, bass.ds(blk, 1), :]).then_inc(raw_out, 16)

            with sp.Fori(0, NG - 1, 1) as i:
                group(i, False)
            group(NG - 1, True)
            norm.load(sp, lambda: sp.wait_ge(in_lo, NB))

        @block.tensor
        def _(pe):
            def group(i):
                for b in range(GB):
                    blk = i * GB + b
                    for c in range(NCH):
                        u = i * (GB * NCH) + b * NCH + c
                        if c == 0:
                            pe.wait_ge(in_lo, blk + 1)
                        pe.wait_ge(hprod, u + 1)
                        s = (b * NCH + c) % 2
                        for half, bank in ((0, pa[s]), (1, pu[s])):
                            n = 0
                            for k in range(KT):
                                for w, a in PASSES:
                                    last = nc.tensor.matmul(bank[:, 0:CH], win[b][w][:, half, k, :],
                                                            K.A[a][:, k, c * CH:(c + 1) * CH],
                                                            start=(n == 0), stop=(n == 3 * KT - 1))
                                    n += 1
                        last.then_inc(au, 1)
                pe.wait_ge(out_lo, i * GB + GB + 1)
                for t in range(NT):
                    pe.wait_ge(h_lo, i * (GB * NCH) + NCH + t // TPC + 2)
                    pe.wait_ge(y_added, i * NT + (2 if t == 0 else t + 1))
                    n = 0
                    for b in range(GB):
                        for a, w in PASSES:
                            for half in range(2):
                                last = nc.tensor.matmul(py[t % 2][:, half * 512:(half + 1) * 512],
                                                        h[a][:, b, t * P:(t + 1) * P],
                                                        wout[w][:, b, half * 512:(half + 1) * 512],
                                                        start=(n == 0), stop=(n == 3 * GB - 1))
                            n += 1
                    last.then_inc(y_ready, 1)

            with pe.Fori(0, NG - 1, 1) as i:
                group(i)
            group(NG - 1)
            if feed:
                feed.turn(pe, lambda c: pe.wait_ge(norm.z, TPC * (c + 1)))

        @block.scalar
        def _(act):
            def split_in(blk, slot):
                act.wait_ge(raw_in, 32 * (blk + 1) if isinstance(blk, int) else blk * 32 + 32)
                nc.scalar.activation(win[slot][0][:], wraw[:], ACT.Copy).then_inc(in_hi, 1)

            split_in(0, 0)

            def group(i, last):
                for b in range(GB):
                    blk = i * GB + b
                    for c in range(NCH):
                        u = i * (GB * NCH) + b * NCH + c
                        s = (b * NCH + c) % 2
                        act.wait_ge(au, u + 1)
                        act.wait_ge(hprod, u + 1)
                        nc.scalar.activation(sa[s][:], pa[s][:, 0:CH], ACT.Silu).then_inc(silu, 1)
                        act.wait_ge(hprod, u + 3)
                        nc.scalar.activation(h[0][:, b, c * CH:(c + 1) * CH], hf[:], ACT.Copy).then_inc(h_hi, 1)
                        if c == 0 and not (last and b == GB - 1):
                            split_in(blk + 1, (b + 1) % 2)
                        if c == 1:
                            act.wait_ge(raw_out, blk * 16 + 16)
                            nc.scalar.activation(wout[0][:, b, :], oraw[:], ACT.Copy).then_inc(out_hi, 1)

            with act.Fori(0, NG - 1, 1) as i:
                group(i, False)
            group(NG - 1, True)
            if feed:
                feed.scale(act)

        @block.vector
        def _(dve):
            dve.sem_inc(hprod, 2)
            dve.sem_inc(y_added, 2)
            dve.sem_inc(out_lo, 1)
            dve.sem_inc(h_lo, 1)

            def split_in(blk, slot):
                dve.wait_ge(in_hi, blk + 1)
                nc.vector.tensor_tensor(win[slot][1][:], wraw[:], win[slot][0][:].bitcast(F32), ALU.subtract).then_inc(in_lo, 1)

            split_in(0, 0)
            dve.wait_ge(y_zero, 1)

            def group(i, last):
                for b in range(GB):
                    blk = i * GB + b
                    for c in range(NCH):
                        u = i * (GB * NCH) + b * NCH + c
                        s = (b * NCH + c) % 2
                        dve.wait_ge(silu, u + 1)
                        dve.wait_ge(h_lo, u + 1)
                        nc.vector.tensor_tensor(hf[:], sa[s][:], pu[s][:, 0:CH], ALU.mult).then_inc(hprod, 1)
                        dve.wait_ge(hprod, u + 3)
                        dve.wait_ge(h_hi, u + 1)
                        nc.vector.tensor_tensor(h[1][:, b, c * CH:(c + 1) * CH], hf[:],
                                                h[0][:, b, c * CH:(c + 1) * CH].bitcast(F32), ALU.subtract).then_inc(h_lo, 1)
                        if c == 0 and not (last and b == GB - 1):
                            split_in(blk + 1, (b + 1) % 2)
                        if c == 1:
                            dve.wait_ge(out_hi, blk + 1)
                            nc.vector.tensor_tensor(wout[1][:, b, :], oraw[:], wout[0][:, b, :].bitcast(F32),
                                                    ALU.subtract).then_inc(out_lo, 1)
                if not last:
                    for t in range(NT):
                        dve.wait_ge(y_ready, i * NT + t + 1)
                        nc.vector.tensor_tensor(Y[:, t, :], Y[:, t, :], py[t % 2][:], ALU.add).then_inc(y_added, 1)

            with dve.Fori(0, NG - 1, 1) as i:
                group(i, False)
            group(NG - 1, True)
            norm.start(dve)
            for t in range(NT + 1):
                if t < NT:
                    dve.wait_ge(y_ready, (NG - 1) * NT + t + 1)
                    nc.vector.tensor_tensor(Y[:, t, :], Y[:, t, :], py[t % 2][:], ALU.add).then_inc(y_added, 1)
                    dve.wait_ge(y_added, (NG - 1) * NT + t + 3)
                    norm.sums(dve, t, Y)
                if t >= 1:
                    norm.unit(dve, t - 1, Y)
            if feed:
                for c in range(NCH):
                    feed.rest(dve, c)

        @block.gpsimd
        def _(gp):
            nc.gpsimd.memset(Y[:], 0.0).then_inc(y_zero, 1)
            norm.pool(gp, Y, lambda g: g.wait_ge(out_lo, NB + 1))


def qkv_phase(nc, K, place, banks):
    NH10 = NH + NKV
    with ExitStack() as ctx:
        sem = lambda n: K.semaphore(f"qkv_{n}")
        W = 256
        pieces = [5 * HGW + m * W for m in range((QW + 2 * KVW) // W)]
        wraw = place("qkv_w_raw", [P, KT, W])
        w = [[place(f"qkv_w_{s}_{x}", [P, KT, W], F32R) for x in ("hi", "lo")] for s in range(2)]
        sq = [place(f"qkv_square_{i}", [P, NH10 * DH]) for i in range(2)]
        ra, rb = place("qkv_rope_a", [P, NH10 * DH]), place("qkv_rope_b", [P, NH10 * DH])
        g = place("qk_norm_rows", [P, 2, DH])
        tab = place("rope_tables", [P, 2, NT, DH])
        ss = place("qkv_square_sums", [P, NT, NH10])
        half = place("qkv_minus_half", [P, NH10])
        raw_in, hi, lo, acc, left = sem("raw"), sem("w_hi"), sem("w_lo"), sem("accumulated"), sem("left_psum")
        consts, squared, summed, rstd, roped, chain, pchain, cached = (
            sem(n) for n in ("consts", "squared", "summed", "rstd", "roped", "chain", "pool_chain", "cache_stored"))
        wv = K.w_mix[0].rearrange("(k p) n -> p k n", p=P)
        block = ctx.enter_context(nc.Block())

        @block.sync
        def _(sp):
            for m, col in enumerate(pieces):
                if m:
                    sp.wait_ge(lo, m)
                sp.dma_start(wraw[:], wv[:, :, col:col + W]).then_inc(raw_in, 16)
                if m == 0:
                    sp.dma_start(g[:, 0, :], K.q_g.broadcast_to([P, DH])).then_inc(consts, 16)
                    sp.dma_start(g[:, 1, :], K.k_g.broadcast_to([P, DH])).then_inc(consts, 16)
                    for i in range(2):
                        sp.dma_start(tab[:, i], K.rope[i].rearrange("(t p) d -> p t d", p=P)).then_inc(consts, 16)
            sp.wait_ge(left, 3 * NT)
            sp.dma_start(K.new_v, K.V[:, CTX_T, :]).then_inc(cached, 16)
            sp.wait_ge(roped, NT)
            sp.dma_start(K.new_k, K.QK[:, CTX_T, QW:]).then_inc(cached, 16)
            sp.wait_ge(cached, 32)

        @block.tensor
        def _(pe):
            for m in range(len(pieces)):
                pe.wait_ge(lo, m + 1)
                for t in range(NT):
                    u = m * NT + t
                    if u >= 4:
                        pe.wait_ge(left, u - 3)
                    n = 0
                    for k in range(KT):
                        for a, x in PASSES:
                            last = nc.tensor.matmul(banks[u % 4][:, 0:W], K.A[a][:, k, t * P:(t + 1) * P],
                                                    w[m % 2][x][:, k, :], start=(n == 0), stop=(n == 3 * KT - 1))
                            n += 1
                    last.then_inc(acc, 1)

        @block.scalar
        def _(act):
            for m in range(len(pieces)):
                act.wait_ge(raw_in, 16 * (m + 1))
                if m >= 2:
                    act.wait_ge(acc, NT * (m - 1))
                nc.scalar.activation(w[m % 2][0][:], wraw[:], ACT.Copy).then_inc(hi, 1)
                if m >= 1:
                    for t in range(NT):
                        u = (m - 1) * NT + t
                        act.wait_ge(acc, u + 1)
                        nc.scalar.copy(K.QK[:, t, (m - 1) * W:m * W], banks[u % 4][:, 0:W]).then_inc(left, 1)
            m = len(pieces) - 1
            for t in range(NT + 1):
                if t < NT:
                    u = m * NT + t
                    act.wait_ge(acc, u + 1)
                    nc.scalar.copy(K.QK[:, t, QW:], banks[u % 4][:, 0:KVW])
                    nc.scalar.copy(K.V[:, t, :], banks[u % 4][:, KVW:W]).then_inc(left, 1)
                    act.wait_ge(left, u + 1)
                    if t >= 2:
                        act.wait_ge(summed, t - 1)
                    nc.scalar.activation(sq[t % 2][:], K.QK[:, t, :], ACT.Square).then_inc(squared, 1)

        @block.gpsimd
        def _(gp):
            link = Chain(gp, pchain)
            link(nc.gpsimd.memset(half[:], -0.5))
            for t in range(NT):
                gp.wait_ge(summed, t + 1)
                link(nc.gpsimd.tensor_scalar(ss[:, t, :], ss[:, t, :], 1.0 / DH, EPS, ALU.mult, ALU.add))
                nc.gpsimd.tensor_tensor(ss[:, t, :], ss[:, t, :], half[:], ALU.pow).then_inc(rstd, 1)

        @block.vector
        def _(dve):
            link = Chain(dve, chain)
            for m in range(len(pieces)):
                dve.wait_ge(hi, m + 1)
                nc.vector.tensor_tensor(w[m % 2][1][:], wraw[:], w[m % 2][0][:].bitcast(F32), ALU.subtract).then_inc(lo, 1)
            dve.wait_ge(consts, 64)

            def normed(t):
                dve.wait_ge(rstd, t + 1)
                x = K.QK[:, t, :].rearrange("p (h d) -> p h d", d=DH)
                link(nc.vector.tensor_tensor(x, x, ss[:, t, :].unsqueeze(2).broadcast_to([P, NH10, DH]), ALU.mult))
                for i, a, b in ((0, 0, NH), (1, NH, NH10)):
                    ins = nc.vector.tensor_tensor(x[:, a:b, :], x[:, a:b, :], g[:, i, :].unsqueeze(1).broadcast_to([P, b - a, DH]), ALU.mult)
                    link(ins)
                cos = tab[:, 0, t, :].unsqueeze(1).broadcast_to([P, NH10, DH])
                A, B = ra[:].rearrange("p (h d) -> p h d", d=DH), rb[:].rearrange("p (h c s e) -> p h c s e", h=NH10, c=2, s=2)
                link(nc.vector.tensor_tensor(A, x, cos, ALU.mult))
                x5 = K.QK[:, t, :].rearrange("p (h c s e) -> p h c s e", h=NH10, c=2, s=2)
                sin = tab[:, 1, t, :].rearrange("p (c s e) -> p c s e", c=2, s=2)
                for s in range(2):
                    link(nc.vector.tensor_tensor(B[:, :, :, s, :], x5[:, :, :, 1 - s, :],
                                                 sin[:, :, s, :].unsqueeze(1).broadcast_to([P, NH10, 2, DH // 4]), ALU.mult))
                nc.vector.tensor_tensor(K.QK[:, t, :], ra[:], rb[:], ALU.add).then_inc(roped, 1)
                dve.wait_ge(roped, t + 1)

            for t in range(NT + 1):
                if t < NT:
                    dve.wait_ge(squared, t + 1)
                    nc.vector.tensor_reduce(ss[:, t, :], sq[t % 2][:].rearrange("p (h d) -> p h d", d=DH), AX_X, ALU.add).then_inc(summed, 1)
                if t >= 1:
                    normed(t - 1)


def attention_phase(nc, K, place, banks):
    HPK = NH // NKV
    with ExitStack() as ctx:
        sem = lambda n: K.semaphore(f"att_{n}")
        NKT = 2 + NT
        LATK = 2 + CTX_T
        SC = DH ** -0.5
        kT = [place(f"kT_{x}", [P, NKT * P], F32R) for x in ("hi", "lo")]
        vs = place("v_hi_lo", [P, NKT, NKV, 2, DH], F32R)
        qs = place("q_stage", [P, HPK, NKV, DH])
        qT = [place(f"qT_{x}", [P, HPK * P], F32R) for x in ("hi", "lo")]
        spare = Plan(nc, K.o_at)
        pr = [[(spare if i == 0 and s < 3 else place)(f"probs_{i}_{s}", [P, LATK * P]) for s in range(HPK)] for i in range(2)]
        assert spare.at <= K.o_at + 4 * HGH * TOK
        pt = [[place(f"probsT_{i}_{x}", [P, HPK * P], F32R) for x in ("hi", "lo")] for i in range(2)]
        ck, cv = place("cache_k_rows", [P, 2, KVW]), place("cache_v_rows", [P, 2, KVW])
        nm = place("neg_max", [P, 2, HPK])
        rsum = place("prob_sums", [P, 2, HPK])
        rinv = place("prob_sum_inverse", [P, HPK])
        rrow = place("inverse_rows", [DH, HPK * P])
        lowh = place("pv_low_half", [DH, HPK * P])
        osum = place("pv_sum", [DH, HPK * P])
        S5 = K.score_banks
        T = [banks[5], banks[6]]
        OB = banks[7]
        cache_in, k_t, k_hi, k_lo, v_hi, v_lo = (sem(n) for n in ("cache_in", "k_turned", "k_hi", "k_lo", "v_hi", "v_lo"))
        q_st, q_t, q_hi, q_lo = (sem(n) for n in ("q_staged", "q_turned", "q_hi", "q_lo"))
        qk, mx, nmx, ex, rc = (sem(n) for n in ("scores", "max", "neg_max", "exp", "inverse"))
        p_t, p_hi, p_lo, pv = (sem(n) for n in ("probs_turned", "probs_hi", "probs_lo", "pv"))
        r_m, r_c, o_low, o_sum, o_out = (sem(n) for n in ("rows_made", "rows_copied", "low_copied", "o_summed", "o_out"))
        block = ctx.enter_context(nc.Block())
        ktile = lambda n: (ck[:, n, :] if n < 2 else K.QK[:, n - 2, QW:])
        kbatches = [list(range(a, min(a + 4, NKT))) for a in range(0, NKT, 4)]

        NU = CTX_T * NKV

        def unit(t, kv):
            if isinstance(t, int) and t == CTX_T:
                return dict(t=t, kv=kv, u=NU + kv, kt=[NKT - 1], b0=NU * LATK + kv)
            u = t * NKV + kv
            return dict(t=t, kv=kv, u=u, kt=list(range(LATK)), b0=u * LATK)

        def cuts(prev):
            n = len(prev["kt"]) if prev else 0
            edges = [-(-n * s // HPK) for s in range(HPK + 1)]
            return [range(edges[s], edges[s + 1]) for s in range(HPK)]

        def run(eng, step):
            step(unit(0, 0), None, None)
            step(unit(0, 1), unit(0, 0), None)
            step(unit(1, 0), unit(0, 1), unit(0, 0))
            with eng.Fori(1, CTX_T - 1, 1) as t:
                step(unit(t, 1), unit(t, 0), unit(t - 1, 1))
                step(unit(t + 1, 0), unit(t, 1), unit(t, 0))
            L = CTX_T - 1
            step(unit(L, 1), unit(L, 0), unit(L - 1, 1))
            step(unit(CTX_T, 0), unit(L, 1), unit(L, 0))
            step(unit(CTX_T, 1), unit(CTX_T, 0), unit(L, 1))
            step(None, unit(CTX_T, 1), unit(CTX_T, 0))
            step(None, None, unit(CTX_T, 1))

        def score_pieces(cur, s):
            if len(cur["kt"]) == 1:
                return [((NKT - 1) * P, P, 1536 * (s % 2))]
            if s % 2 == 0:
                return [(0, 512, 0), (512, 512, 512), (1024, 256, 1024)]
            return [(256, 512, 1536), (768, 512, 2048), (0, 256, 1280)]

        def score_view(cur, s):
            if len(cur["kt"]) == 1:
                return S5[:, 1536 * (s % 2):1536 * (s % 2) + P]
            return S5[:, 1280 * (s % 2):1280 * (s % 2) + LATK * P]

        def needs_queries(cur):
            return cur is not None and cur["kv"] == 0

        @block.sync
        def _(sp):
            sp.dma_start(ck[:], K.cache_k.rearrange("(t p) h d -> p t (h d)", p=P)).then_inc(cache_in, 16)
            sp.dma_start(cv[:], K.cache_v.rearrange("(t p) h d -> p t (h d)", p=P)).then_inc(cache_in, 16)

        @block.tensor
        def _(pe):
            pe.wait_ge(cache_in, 32)
            for n, batch in enumerate(kbatches):
                if n >= 2:
                    pe.wait_ge(k_lo, n - 1)
                for i, kt in enumerate(batch):
                    last = nc.tensor.transpose(T[n % 2][:, i * P:(i + 1) * P], ktile(kt), K.ident[:])
                last.then_inc(k_t, 1)
            pe.wait_ge(k_lo, len(kbatches))
            pe.wait_ge(v_lo, 2)

            def values(prev, n):
                pe.wait_ge(p_lo, prev["b0"] + n + 3)
                if n == 0:
                    pe.wait_ge(o_sum, prev["u"] + 1)
                cnt = len(prev["kt"])
                for x in range(2):
                    last = nc.tensor.matmul(OB, vs[:, prev["kt"][n], prev["kv"]].rearrange("p x d -> p (x d)"), pt[n % 2][x][:],
                                            start=(n == 0 and x == 0), stop=(n == cnt - 1 and x == 1))
                last.then_inc(pv, 1)

            def turn(prev, n):
                if n == 0:
                    pe.wait_ge(ex, (prev["u"] + 1) * HPK + 2)
                    pe.wait_ge(p_lo, prev["b0"] + 2)
                else:
                    pe.wait_ge(p_lo, prev["b0"] + n + 1)
                if n == 1:
                    pe.wait_ge(r_c, prev["u"] + 1)
                for j in range(HPK):
                    last = nc.tensor.transpose(T[n % 2][:, j * P:(j + 1) * P],
                                               pr[prev["kv"]][j][:, n * P:(n + 1) * P], K.ident[:])
                last.then_inc(p_t, 1)
                if n >= 1:
                    values(prev, n - 1)

            def step(cur, prev, fin):
                if needs_queries(cur):
                    pe.wait_ge(q_st, cur["t"] + 1)
                    for j in range(HPK):
                        last = nc.tensor.transpose(T[0][:, j * P:(j + 1) * P], qs[:, j].rearrange("p k d -> p (k d)"), K.ident[:])
                    last.then_inc(q_t, 1)
                    pe.wait_ge(q_lo, cur["t"] + 1)
                for s, blocks in enumerate(cuts(prev)):
                    if cur:
                        a0, a1 = cur["kv"] * DH, (cur["kv"] + 1) * DH
                        for i, (key, width, col) in enumerate(score_pieces(cur, s)):
                            if i == 0:
                                pe.wait_ge(ex, cur["u"] * HPK + s + 1)
                            if i == 2:
                                pe.wait_ge(ex, cur["u"] * HPK + s + 2)
                            for n, (a, b) in enumerate(PASSES):
                                last = nc.tensor.matmul(S5[:, col:col + width], qT[a][a0:a1, s * P:(s + 1) * P],
                                                        kT[b][a0:a1, key:key + width], start=(n == 0), stop=(n == 2))
                        last.then_inc(qk, 1)
                    if prev:
                        for n in blocks:
                            turn(prev, n)
                if prev:
                    values(prev, len(prev["kt"]) - 1)
                    pe.wait_ge(rc, prev["u"] + 1)
                    pe.wait_ge(r_c, prev["u"] + 1)
                    for j in range(HPK):
                        last = nc.tensor.matmul(T[1][0:DH, j * P:(j + 1) * P], rinv[:, j:j + 1].broadcast_to([P, DH]),
                                                K.ident[:], start=True, stop=True)
                    last.then_inc(r_m, 1)

            run(pe, step)

        @block.scalar
        def _(act):
            act.sem_inc(ex, 2)
            act.sem_inc(r_c, 1)
            act.wait_ge(cache_in, 32)
            nc.scalar.activation(vs[:, 0:2, :, 0, :], cv[:].rearrange("p t (h d) -> p t h d", h=NKV), ACT.Copy).then_inc(v_hi, 1)
            nc.scalar.activation(vs[:, 2:NKT, :, 0, :], K.V[:].rearrange("p t (h d) -> p t h d", h=NKV), ACT.Copy).then_inc(v_hi, 1)
            for n, batch in enumerate(kbatches):
                act.wait_ge(k_t, n + 1)
                c0, wd = batch[0] * P, len(batch) * P
                nc.scalar.activation(kT[0][:, c0:c0 + wd], T[n % 2][:, 0:wd], ACT.Copy).then_inc(k_hi, 1)

            def step(cur, prev, fin):
                if needs_queries(cur):
                    act.wait_ge(q_t, cur["t"] + 1)
                    nc.scalar.activation(qT[0][:], T[0], ACT.Copy).then_inc(q_hi, 1)
                for s, blocks in enumerate(cuts(prev)):
                    for n in blocks:
                        act.wait_ge(p_t, prev["b0"] + n + 1)
                        act.wait_ge(pv, prev["b0"] + (n + 1 if len(prev["kt"]) > 1 else 2))
                        nc.scalar.activation(pt[n % 2][0][:], T[n % 2], ACT.Copy).then_inc(p_hi, 1)
                    if cur:
                        act.wait_ge(nmx, cur["u"] * HPK + s + 1)
                        nc.scalar.activation(pr[cur["kv"]][s][:, 0:len(cur["kt"]) * P], score_view(cur, s), ACT.Exp,
                                             bias=nm[:, cur["kv"], s:s + 1], scale=SC,
                                             accum_out=rsum[:, cur["kv"], s:s + 1]).then_inc(ex, 1)
                if prev:
                    act.wait_ge(r_m, prev["u"] + 2)
                    act.wait_ge(o_out, prev["u"] + 1)
                    nc.scalar.copy(rrow[:], T[1][0:DH, :]).then_inc(r_c, 1)
                    act.wait_ge(pv, prev["b0"] + len(prev["kt"]) + 2)
                    nc.scalar.copy(lowh[:], OB[DH:P, :]).then_inc(o_low, 1)

            run(act, step)

        @block.vector
        def _(dve):
            for s, credit in ((p_lo, 2), (pv, 2), (o_sum, 1), (r_m, 1), (o_out, 1)):
                dve.sem_inc(s, credit)
            dve.wait_ge(v_hi, 2)
            nc.vector.tensor_tensor(vs[:, 0:2, :, 1, :], cv[:].rearrange("p t (h d) -> p t h d", h=NKV),
                                    vs[:, 0:2, :, 0, :].bitcast(F32), ALU.subtract).then_inc(v_lo, 1)
            nc.vector.tensor_tensor(vs[:, 2:NKT, :, 1, :], K.V[:].rearrange("p t (h d) -> p t h d", h=NKV),
                                    vs[:, 2:NKT, :, 0, :].bitcast(F32), ALU.subtract).then_inc(v_lo, 1)
            for n, batch in enumerate(kbatches):
                dve.wait_ge(k_hi, n + 1)
                c0, wd = batch[0] * P, len(batch) * P
                nc.vector.tensor_tensor(kT[1][:, c0:c0 + wd], T[n % 2][:, 0:wd], kT[0][:, c0:c0 + wd].bitcast(F32),
                                        ALU.subtract).then_inc(k_lo, 1)

            def stage(t):
                if not (isinstance(t, int) and t == 0):
                    dve.wait_ge(q_t, t)
                q4 = K.QK[:, bass.ds(t, 1), 0:QW].rearrange("p o (k j d) -> p o k j d", k=NKV, j=HPK)
                for kv in range(NKV):
                    ins = nc.vector.tensor_copy(qs[:, :, kv, :], q4[:, 0, kv, :, :])
                ins.then_inc(q_st, 1)

            def step(cur, prev, fin):
                if needs_queries(cur):
                    stage(cur["t"])
                    dve.wait_ge(q_hi, cur["t"] + 1)
                    nc.vector.tensor_tensor(qT[1][:], T[0], qT[0][:].bitcast(F32), ALU.subtract).then_inc(q_lo, 1)
                for s, blocks in enumerate(cuts(prev)):
                    if prev and s == 0:
                        dve.wait_ge(ex, (prev["u"] + 1) * HPK + 2)
                        dve.wait_ge(r_m, prev["u"] + 1)
                        nc.vector.reciprocal(rinv[:], rsum[:, prev["kv"], :]).then_inc(rc, 1)
                    if cur:
                        h = cur["u"] * HPK + s
                        dve.wait_ge(qk, h + 1)
                        m = nm[:, cur["kv"], s:s + 1]
                        nc.vector.reduce_max(m, score_view(cur, s), AX_X).then_inc(mx, 1)
                        dve.wait_ge(mx, h + 1)
                        nc.vector.tensor_scalar(m, m, -SC, None, ALU.mult).then_inc(nmx, 1)
                    if fin and s == 0:
                        dve.wait_ge(o_low, fin["u"] + 1)
                        nc.vector.tensor_tensor(osum[:], OB[0:DH, :], lowh[:], ALU.add).then_inc(o_sum, 1)
                        dve.wait_ge(o_sum, fin["u"] + 2)
                        dve.wait_ge(r_c, fin["u"] + 2)
                        kt0 = HGH + 2 * fin["kv"]
                        for par in range(2):
                            v = lambda x: x[:].rearrange("p (a b q) -> p a b q", b=2, q=P)[:, :, par, :]
                            last = nc.vector.tensor_tensor(K.O[par * DH:(par + 1) * DH, kt0:kt0 + 2, bass.ds(fin["t"] * P, P)],
                                                           v(osum), v(rrow), ALU.mult)
                        last.then_inc(o_out, 1)
                        dve.wait_ge(o_out, fin["u"] + 2)
                    for n in blocks:
                        dve.wait_ge(p_hi, prev["b0"] + n + 1)
                        nc.vector.tensor_tensor(pt[n % 2][1][:], T[n % 2], pt[n % 2][0][:].bitcast(F32),
                                                ALU.subtract).then_inc(p_lo, 1)

            run(dve, step)


def view_chunks(x):
    return x[:].rearrange("p (c s) -> p c s", s=SCAN)


def hgrn_phase(nc, K, place, banks):
    with ExitStack() as ctx:
        sem = lambda n: K.semaphore(f"scan_{n}")
        raw = place("scan_w_raw", [P, KT, P])
        W = [[place(f"scan_w_{s}_{x}", [P, KT, P], F32R) for x in ("hi", "lo")] for s in range(2)]
        q, acc = place("scan_q", [P, TOK]), place("scan_out", [P, TOK])
        v, v_next = place("scan_v", [P, NT, P]), place("scan_v_next", [P, NT, P])
        B = [[place(f"scan_buf_{d}_{i}", [P, TOK]) for i in range(4)] for d in range(2)]
        kb = place("ke_blocks", [P, 4, 4, P])
        S = place("states", [P, NSC, P])
        am = [place(f"weights_{i}", [P, 4 * P]) for i in range(2)]
        reset = place("scan_reset", [P, CH])
        mask = [place(f"mask_{d}", [P, P]) for d in range(2)]
        ones = place("ones", [P, P])
        zero = place("zero_state", [P, P])
        init = [place(f"init_state_{d}", [P, P]) for d in range(2)]
        fin = [place(f"final_state_{d}", [P, P]) for d in range(2)]
        sc = [place(f"chunk_sums_{d}", [P, 3, NSC]) for d in range(2)]
        lb = place("lower_bounds", [P, 3, 2, HGH])
        cur = place("head_cols", [P, 7])
        proj, tr, ub, ab, ob = banks[0:3], banks[3], banks[4:6], banks[6], banks[7]
        (raw_in, w_hi, w_lo, acc_p, left, lbs, ready, head, v_ok) = (
            sem(n) for n in ("w_loaded", "w_hi", "w_lo", "projected", "left_psum", "lb_ready", "consts_ready", "head_cols", "v_ready"))
        (logf, sums, sums_e, dev, e_dev, factors) = (
            sem(n) for n in ("logf", "sums", "sums_exp", "deviation", "deviation_exp", "factors"))
        (kt_s, kb_s, a_s, am_s, u_s, st_s, o_s, oe_s) = (
            sem(n) for n in ("ke_turned", "ke_blocks", "weights", "weights_masked", "updates", "states", "out", "out_taken"))
        (init_in, fin_s, sq_s, ss_s, ms_s, rs_s) = (
            sem(n) for n in ("init_loaded", "final_ready", "squares", "square_sums", "mean_squares", "rstd"))
        stored, chain, pchain = sem("states_stored"), sem("chain"), sem("pool_chain")
        wv = K.w_mix[0].rearrange("(k p) n -> p k n", p=P)
        V_, G_, Q_, F0, F1 = range(5)
        COLS = [HGW, 4 * HGW, 0, 2 * HGW, 3 * HGW]
        FIRST = [0, NT, NT + NCH, NT + 2 * NCH, NT + 3 * NCH]
        NBLK, NU = len(COLS), NT + 4 * NCH
        block_of = lambda u: max(b for b in range(NBLK) if FIRST[b] <= u)
        rounds = [[[0, 1, 2, 3], [4, 5, 6, 7], [8]], [[7, 6, 5, 4], [3, 2, 1, 0], [8]]]
        RPH, TPH = 6, 2 * NT
        CPT = P // SCAN
        fill = [[range(0, 3), range(3, 6), range(6, 9)], [range(9, 10), range(10, 11), ()], [range(11, 12), (), ()],
                [range(12, 13), range(13, 14), range(14, 15)], [range(15, 16), range(16, 17), range(17, 18)],
                [range(18, 19), (), range(19, 20)]]
        TAIL = range(20, 21)

        def before(d, c):
            if c == (0, LSC - 1)[d]:
                return init[d][:]
            if c == (LSC, NSC - 1)[d]:
                return zero[:]
            return S[:, c, :]

        def after(d, c):
            if c == (LSC - 1, 0)[d]:
                return None
            if c == (NSC - 1, LSC)[d]:
                return fin[d][:]
            return S[:, c + (1, -1)[d], :]

        block = ctx.enter_context(nc.Block())

        @block.sync
        def _(sp):
            def initial(h):
                for d, src in enumerate((K.state_f, K.state_b)):
                    sp.dma_start(init[d][:], src[bass.ds(h, 1)].rearrange("o k v -> (o k) v")).then_inc(init_in, 16)

            def final(h):
                for d, dst in enumerate((K.new_f, K.new_b)):
                    sp.dma_start(dst[bass.ds(h, 1)].rearrange("o k v -> (o k) v"), fin[d][:]).then_inc(stored, 16)

            initial(0)
            for b, col in enumerate(COLS):
                sp.wait_ge(w_lo, b + 1)
                sp.dma_start(raw[:], wv[:, :, col:col + P]).then_inc(raw_in, 16)
            with sp.Fori(2, HGH + 1, 1) as n:
                for b, col in enumerate(COLS):
                    sp.wait_ge(w_lo, n * NBLK + (b + 1 - NBLK))
                    sp.dma_start(raw[:], wv[:, :, bass.ds(n * P + (col - P), P)]).then_inc(raw_in, 16)
                sp.wait_ge(fin_s, n * 2 - 2)
                final(n - 2)
                sp.wait_ge(o_s, n * RPH + (2 - RPH))
                initial(n - 1)
            sp.wait_ge(fin_s, 2 * HGH)
            final(HGH - 1)
            sp.wait_ge(stored, HGH * 32 + 32)

        @block.gpsimd
        def _(gp):
            link = Chain(gp, pchain)
            link(nc.gpsimd.memset(kb[:], 0.0))
            link(nc.gpsimd.memset(zero[:], 0.0))
            link(nc.gpsimd.memset(ones[:], 1.0))
            link(nc.gpsimd.memset(reset[:], 1.0))
            link(nc.gpsimd.memset(view_chunks(reset)[:, :, 0:1], 0.0))
            for d in range(2):
                m3 = view_chunks(mask[d])
                link(nc.gpsimd.memset(mask[d][:], 1.0))
                link(nc.gpsimd.affine_select(out=m3, in_=m3, compare_op=ALU.is_ge, fill=0.0, base=0,
                                             pattern=[[-SCAN, CPT], [0, SCAN]], channel_multiplier=1))
                link(nc.gpsimd.affine_select(out=m3, in_=m3, compare_op=ALU.is_ge, fill=0.0, base=SCAN - 1,
                                             pattern=[[SCAN, CPT], [0, SCAN]], channel_multiplier=-1))
                s = (1, -1)[d]
                link(nc.gpsimd.affine_select(out=mask[d][:], in_=mask[d][:], compare_op=ALU.is_ge, fill=0.0, base=0,
                                             pattern=[[s, P]], channel_multiplier=-s))
            gp.sem_inc(ready, 1)

        @block.tensor
        def _(pe):
            pe.wait_ge(ready, 1)

            def output(h, u):
                b = block_of(u)
                i, slot = u - FIRST[b], b % 2
                if i == 0:
                    pe.wait_ge(w_lo, h * NBLK + b + 2)
                pe.wait_ge(left, h * NU + u + 1)
                n = 0
                for k in range(KT):
                    for x, y in PASSES:
                        if b == V_:
                            last = nc.tensor.matmul(proj[u % 3][:, 0:P], K.A[x][:, k, i * P:(i + 1) * P],
                                                    W[slot][y][:, k, :], start=(n == 0), stop=(n == 3 * KT - 1))
                        else:
                            last = nc.tensor.matmul(proj[u % 3][:, 0:CH], W[slot][x][:, k, :],
                                                    K.A[y][:, k, i * CH:(i + 1) * CH], start=(n == 0), stop=(n == 3 * KT - 1))
                        n += 1
                last.then_inc(acc_p, 1)

            def turn(h, d, r):
                R = h * RPH + 3 * d + r
                if r == 0:
                    pe.wait_ge(factors, h * 2 + d + 1)
                pe.wait_ge(kb_s, R + 1)
                for j, t in enumerate(rounds[d][r]):
                    last = nc.tensor.transpose(tr[:, j * P:(j + 1) * P], B[d][0][:, t * P:(t + 1) * P], K.ident[:])
                last.then_inc(kt_s, 1)

            def scan_round(h, d, r, nxt):
                _, Bq, Bi, Bd = B[d]
                tiles = rounds[d][r]
                R = h * RPH + 3 * d + r
                gaps = fill[3 * d + r] if nxt is not None else [(), (), ()]
                if (d, r) != (1, 2):
                    turn(h, d, r)
                pe.wait_ge(am_s, R + 1)
                for j, t in enumerate(tiles):
                    last = nc.tensor.matmul(ab[:, j * P:(j + 1) * P], Bd[:, t * P:(t + 1) * P], Bq[:, t * P:(t + 1) * P],
                                            start=True, stop=True)
                last.then_inc(a_s, 1)
                for u in gaps[0]:
                    output(nxt, u)
                if (d, r) == (0, 0):
                    pe.wait_ge(v_ok, h + 2)
                pe.wait_ge(kb_s, R + 2)
                for j, t in enumerate(tiles):
                    p = NT * d + 4 * r + j
                    pe.wait_ge(st_s, h * TPH + p + 1)
                    for c in range(CPT):
                        last = nc.tensor.matmul(ub[p % 2][:, c * P:(c + 1) * P], kb[:, j, c, :], v[:, t, :],
                                                start=True, stop=True)
                    last.then_inc(u_s, 1)
                    if j == 1:
                        for u in gaps[1]:
                            output(nxt, u)
                if (d, r) == (1, 1):
                    turn(h, 1, 2)
                for u in gaps[2]:
                    output(nxt, u)
                if r == 0:
                    pe.wait_ge(init_in, h * 32 + 32)
                pe.wait_ge(am_s, R + 2)
                pe.wait_ge(oe_s, R + 1)
                for j, t in enumerate(tiles):
                    p = NT * d + 4 * r + j
                    pe.wait_ge(st_s, h * TPH + p + 3)
                    nc.tensor.matmul(ob[:, j * P:(j + 1) * P], v[:, t, :], am[(3 * d + r) % 2][:, j * P:(j + 1) * P],
                                     start=True, stop=False)
                    for c in range(CPT):
                        a = j * P + c * SCAN
                        last = nc.tensor.matmul(ob[:, a:a + SCAN], before(d, t * CPT + c),
                                                Bi[:, t * P + c * SCAN:t * P + (c + 1) * SCAN],
                                                start=False, stop=(c == CPT - 1))
                last.then_inc(o_s, 1)

            def scan_head(h, nxt):
                for d in range(2):
                    for r in range(3):
                        scan_round(h, d, r, nxt)
                pe.wait_ge(sq_s, h + 1)
                for c, bank in enumerate((tr, ub[0], ub[1])):
                    nc.tensor.matmul(bank[:, 0:CH], ones[:], B[1][1][:, c * CH:(c + 1) * CH],
                                     start=True, stop=True).then_inc(ss_s, 1)
                if nxt is not None:
                    for u in TAIL:
                        output(nxt, u)
                pe.wait_ge(ms_s, h * NCH + NCH)

            for u in range(NU):
                output(0, u)
            with pe.Fori(0, HGH - 1, 1) as h:
                scan_head(h, h + 1)
            scan_head(HGH - 1, None)

        @block.scalar
        def _(act):
            act.sem_inc(left, 3)
            act.sem_inc(kb_s, 1)
            act.wait_ge(lbs, 1)
            for d in range(2):
                nc.scalar.activation(lb[:, 0, d, :], K.lbd[:, d, :], ACT.Sigmoid)
                last = nc.scalar.activation(lb[:, 1, d, :], K.lbd[:, d, :], ACT.Sigmoid, scale=-1.0)
            last.then_inc(lbs, 1)

            def evacuate(h, outputs):
                for u in outputs:
                    b = block_of(u)
                    i = u - FIRST[b]
                    act.wait_ge(acc_p, h * NU + u + 1)
                    if b == V_:
                        if i == 0:
                            act.wait_ge(v_ok, h + 1)
                        ins = nc.scalar.copy(v_next[:, i, :], proj[u % 3][:, 0:P])
                    else:
                        cols = slice(i * CH, (i + 1) * CH)
                        dst = (K.O[:, bass.ds(h, 1), cols].rearrange("p o t -> p (o t)") if b == G_
                               else {Q_: q, F0: B[0][0], F1: B[1][0]}[b][:, cols])
                        ins = nc.scalar.activation(dst, proj[u % 3][:, 0:CH], ACT.Sigmoid if b >= F0 else ACT.Silu)
                    ins.then_inc(left, 1)

            def split(h, b):
                act.wait_ge(raw_in, h * (NBLK * 16) + (b * 16 + 16))
                if b >= 2:
                    act.wait_ge(acc_p, h * NU + FIRST[b - 1])
                elif b == 0 and not (isinstance(h, int) and h == 0):
                    act.wait_ge(acc_p, h * NU)
                nc.scalar.activation(W[b % 2][0][:], raw[:], ACT.Copy).then_inc(w_hi, 1)

            def log_gate(h, d):
                act.wait_ge(left, h * NU + FIRST[F0 + d] + NCH + 3)
                act.wait_ge(head, h + 1)
                nc.scalar.activation(B[d][1][:], B[d][0][:], ACT.Ln, bias=cur[:, d:d + 1], scale=cur[:, 2 + d:3 + d]).then_inc(logf, 1)

            def exps(h, d):
                act.wait_ge(sums, h * 2 + d + 1)
                act.wait_ge(dev, h * 2 + d + 1)
                nc.scalar.activation(sc[d][:], sc[d][:], ACT.Exp).then_inc(sums_e, 1)
                nc.scalar.activation(B[d][1][:], B[d][2][:], ACT.Exp)
                nc.scalar.activation(B[d][3][:], B[d][2][:], ACT.Exp, scale=-1.0).then_inc(e_dev, 1)

            def blocks(h, d, r):
                tiles = rounds[d][r]
                R = h * RPH + 3 * d + r
                act.wait_ge(kt_s, R + 1)
                act.wait_ge(u_s, h * TPH + NT * d + 4 * r + 1)
                for c in range(CPT):
                    rows = slice(c * SCAN, (c + 1) * SCAN)
                    last = nc.scalar.copy(kb[rows, 0:len(tiles), c, :],
                                          tr[rows, 0:len(tiles) * P].rearrange("p (j k) -> p j k", k=P))
                last.then_inc(kb_s, 1)

            def scan_head(h, nxt):
                some = lambda f, *a: f(nxt, *a) if nxt is not None else None
                some(split, 0)
                blocks(h, 0, 0)
                some(split, 1)
                some(evacuate, fill[0][0])
                log_gate(h, 1)
                some(evacuate, fill[0][1])
                exps(h, 1)
                some(evacuate, fill[0][2])
                blocks(h, 0, 1)
                some(split, 2)
                some(evacuate, [*fill[1][0], *fill[1][1]])
                blocks(h, 0, 2)
                some(evacuate, fill[2][0])
                some(split, 3)
                blocks(h, 1, 0)
                some(evacuate, [u for f in fill[3] for u in f])
                some(split, 4)
                blocks(h, 1, 1)
                some(evacuate, fill[4][0])
                some(evacuate, fill[4][1])
                blocks(h, 1, 2)
                some(evacuate, fill[4][2])
                some(log_gate, 0)
                some(evacuate, fill[5][0])
                some(exps, 0)
                some(evacuate, fill[5][2])
                act.wait_ge(oe_s, h * RPH + RPH + 1)
                nc.scalar.activation(B[1][1][:], acc[:], ACT.Square).then_inc(sq_s, 1)
                act.wait_ge(ms_s, h * NCH + NCH)
                nc.scalar.activation(B[1][3][:], B[1][3][:], ACT.Ln).then_inc(rs_s, 1)
                act.wait_ge(rs_s, h * 2 + 1)
                nc.scalar.activation(B[1][3][:], B[1][3][:], ACT.Exp, scale=-0.5).then_inc(rs_s, 1)
                some(evacuate, TAIL)

            split(0, 0)
            split(0, 1)
            for b in range(NBLK):
                evacuate(0, range(FIRST[b], (FIRST + [NU])[b + 1]))
                if b + 2 < NBLK:
                    split(0, b + 2)
                if b == F0:
                    log_gate(0, 0)
                    exps(0, 0)
            with act.Fori(0, HGH - 1, 1) as h:
                scan_head(h, h + 1)
            scan_head(HGH - 1, None)

        @block.vector
        def _(dve):
            for s, credit in ((w_lo, 1), (am_s, 1), (st_s, 2), (o_s, 2), (oe_s, 1), (u_s, 1), (stored, 32), (v_ok, 1)):
                dve.sem_inc(s, credit)
            dve.sem_inc(lbs, 1)
            dve.wait_ge(lbs, 2)
            nc.vector.tensor_scalar(lb[:, 2], lb[:, 1], -1.0, None, ALU.mult).then_inc(lbs, 1)
            dve.wait_ge(lbs, 3)
            link = LoopChain(dve, chain)
            rev = lambda x: x[:, ::-1]

            def split(h, b):
                dve.wait_ge(w_hi, h * NBLK + b + 1)
                nc.vector.tensor_tensor(W[b % 2][1][:], raw[:], W[b % 2][0][:].bitcast(F32), ALU.subtract).then_inc(w_lo, 1)

            def columns(h):
                for i in range(3):
                    for d in range(2):
                        ins = nc.vector.tensor_copy(cur[:, 2 * i + d:2 * i + d + 1], lb[:, i, d, bass.ds(h, 1)])
                        link(ins)
                dve.sem_inc(head, 1)

            def gates(h, d):
                Bk, Bl, Bg, _ = B[d]
                dve.wait_ge(logf, h * 2 + d + 1)
                link(nc.vector.tensor_scalar(Bk[:], Bk[:], cur[:, 4 + d:5 + d], cur[:, 2 + d:3 + d], ALU.mult, ALU.add))
                for c in range(NCH):
                    a = c * CH
                    src, dst = Bl[:, a:a + CH], Bg[:, a:a + CH]
                    if d:
                        src, dst = rev(src), rev(dst)
                    ins = nc.vector.tensor_tensor_scan(dst, reset[:], src, 0.0, ALU.mult, ALU.add)
                link(ins)
                g3 = view_chunks(Bg)
                mid, end = (SCAN // 2 - 1, SCAN - 1) if d == 0 else (SCAN // 2, 0)
                nc.vector.tensor_copy(sc[d][:, 0, :], g3[:, :, mid])
                link(nc.vector.tensor_copy(sc[d][:, 1, :], g3[:, :, end]))
                nc.vector.tensor_tensor(sc[d][:, 2, :], sc[d][:, 1, :], sc[d][:, 0, :], ALU.subtract).then_inc(sums, 1)
                nc.vector.tensor_tensor(g3, g3, sc[d][:, 0, :].unsqueeze(2).broadcast_to([P, NSC, SCAN]), ALU.subtract).then_inc(dev, 1)

            def products(h, d):
                Bk, Bq, Bi, Bd = B[d]
                dve.wait_ge(sums_e, h * 2 + d + 1)
                dve.wait_ge(e_dev, h * 2 + d + 1)
                dve.wait_ge(left, h * NU + FIRST[Q_] + NCH + 3)
                bc = lambda i: sc[d][:, i, :].unsqueeze(2).broadcast_to([P, NSC, SCAN])
                nc.vector.tensor_tensor(Bq[:], q[:], Bq[:], ALU.mult)
                link(nc.vector.tensor_tensor(Bd[:], Bk[:], Bd[:], ALU.mult))
                nc.vector.tensor_tensor(view_chunks(Bi), view_chunks(Bq), bc(0), ALU.mult)
                nc.vector.tensor_tensor(view_chunks(Bk), view_chunks(Bd), bc(2), ALU.mult).then_inc(factors, 1)

            def take_out(h, d, r):
                tiles = rounds[d][r]
                R = h * RPH + 3 * d + r
                dve.wait_ge(o_s, R + 3)
                if d == 0:
                    lo = tiles[0] * P
                    nc.vector.tensor_copy(acc[:, lo:lo + len(tiles) * P], ob[:, 0:len(tiles) * P]).then_inc(oe_s, 1)
                else:
                    lo = tiles[-1] * P
                    a3 = acc[:, lo:lo + len(tiles) * P].rearrange("p (j k) -> p j k", k=P)[:, ::-1, :]
                    o3 = ob[:, 0:len(tiles) * P].rearrange("p (j k) -> p j k", k=P)
                    nc.vector.tensor_tensor(a3, o3, a3, ALU.add).then_inc(oe_s, 1)
                dve.wait_ge(oe_s, R + 2)

            def masked(h, d, r):
                n = len(rounds[d][r])
                R = h * RPH + 3 * d + r
                dve.wait_ge(a_s, R + 1)
                dve.wait_ge(o_s, R + 1)
                nc.vector.tensor_tensor(am[(3 * d + r) % 2][:, 0:n * P].rearrange("p (j i) -> p j i", i=P),
                                        ab[:, 0:n * P].rearrange("p (j i) -> p j i", i=P),
                                        mask[d][:].unsqueeze(1).broadcast_to([P, n, P]), ALU.mult).then_inc(am_s, 1)

            def states(h, d, r, js):
                for j in js:
                    t = rounds[d][r][j]
                    p = NT * d + 4 * r + j
                    dve.wait_ge(u_s, h * TPH + p + 2)
                    for c in range(CPT) if d == 0 else range(CPT - 1, -1, -1):
                        n = t * CPT + c
                        if after(d, n) is not None:
                            link(nc.vector.scalar_tensor_tensor(after(d, n), before(d, n), sc[d][:, 1, n:n + 1],
                                                                ub[p % 2][:, c * P:(c + 1) * P], ALU.mult, ALU.add))
                    dve.sem_inc(st_s, 1)

            def norm(h):
                for c, bank in enumerate((tr, ub[0], ub[1])):
                    dve.wait_ge(ss_s, h * NCH + c + 1)
                    nc.vector.tensor_scalar(B[1][3][:, c * CH:(c + 1) * CH], bank[:, 0:CH], 1.0 / P, EPS,
                                            ALU.mult, ALU.add).then_inc(ms_s, 1)
                link(nc.vector.tensor_copy(cur[:, 6:7], K.cols[:, bass.ds(h + C_HGN, 1)]))
                dve.wait_ge(rs_s, h * 2 + 2)
                link(nc.vector.scalar_tensor_tensor(acc[:], acc[:], cur[:, 6:7], B[1][3][:], ALU.mult, ALU.mult))
                out = K.O[:, bass.ds(h, 1), :].rearrange("p o t -> p (o t)")
                link(nc.vector.tensor_tensor(out, acc[:], out, ALU.mult))

            def scan_head(h, nxt):
                some = lambda f, *a: f(nxt, *a) if nxt is not None else None
                dve.wait_ge(left, h * NU + NT + 3)
                nc.vector.tensor_copy(v[:], v_next[:]).then_inc(v_ok, 1)
                some(split, 0)
                masked(h, 0, 0)
                some(split, 1)
                dve.wait_ge(stored, h * 32 + 32)
                dve.wait_ge(init_in, h * 32 + 32)
                states(h, 0, 0, (0, 1))
                gates(h, 1)
                states(h, 0, 0, (2, 3))
                masked(h, 0, 1)
                take_out(h, 0, 0)
                some(split, 2)
                states(h, 0, 1, (0, 1))
                products(h, 1)
                states(h, 0, 1, (2, 3))
                masked(h, 0, 2)
                take_out(h, 0, 1)
                states(h, 0, 2, (0,))
                dve.sem_inc(fin_s, 1)
                some(split, 3)
                take_out(h, 0, 2)
                masked(h, 1, 0)
                states(h, 1, 0, (0, 1, 2, 3))
                some(split, 4)
                masked(h, 1, 1)
                take_out(h, 1, 0)
                states(h, 1, 1, (0, 1, 2, 3))
                some(columns)
                masked(h, 1, 2)
                take_out(h, 1, 1)
                states(h, 1, 2, (0,))
                dve.sem_inc(fin_s, 1)
                some(gates, 0)
                take_out(h, 1, 2)
                some(products, 0)
                norm(h)

            link.begin(0, 0)
            split(0, 0)
            split(0, 1)
            columns(0)
            for b in range(2, NBLK):
                split(0, b)
            gates(0, 0)
            products(0, 0)
            first = link.n
            with dve.Fori(0, HGH - 1, 1) as h:
                link.begin(h, K.scan_links, first)
                scan_head(h, h + 1)
                link.end()
            link.begin(HGH - 1, K.scan_links, first)
            scan_head(HGH - 1, None)


def mix_out_phase(nc, K, place, banks):
    with ExitStack() as ctx:
        sem = lambda n: K.semaphore(f"mixout_{n}")
        Y = K.Y
        wo = [place(f"mixout_w_{x}", [P, KT, D], F32R) for x in ("hi", "lo")]
        raw = [place(f"mixout_w_raw_{i}", [P, D]) for i in range(2)]
        tmp = [place(f"mixout_tmp_{i}", [P, CH]) for i in range(2)]
        gB, bB, xo = (place(f"mixout_{n}", [P, D]) for n in ("ln_g_rows", "ln_b_rows", "x_row"))
        norm = Norm(K, ctx, nc, "mixout", place, 1, 5, K.x1_rows, K.x2_rows, gB[:], bB[:], xo[:])
        feed = Feed(K, ctx, nc, "mixout", Y, tmp, banks[0:4], 7, 6)
        py = K.wide[2:4]
        raw_in = [sem("w_loaded_even"), sem("w_loaded_odd")]
        w_hi, w_lo, o_hi, o_lo, y_ready, y_taken = (sem(n) for n in ("w_hi", "w_lo", "o_hi", "o_lo", "y_ready", "y_taken"))
        wv = K.w_mix_out[0].rearrange("(k p) n -> p k n", p=P)
        block = ctx.enter_context(nc.Block())

        @block.sync
        def _(sp):
            for k in range(KT):
                if k >= 2:
                    sp.wait_ge(w_lo, k - 1)
                sp.dma_start(raw[k % 2][:], wv[:, k, :]).then_inc(raw_in[k % 2], 16)
            norm.load(sp, lambda: None)

        @block.tensor
        def _(pe):
            pe.wait_ge(o_lo, KT)
            for t in range(NT):
                if t >= 2:
                    pe.wait_ge(y_taken, t - 1)
                n = 0
                for k in range(KT):
                    if t == 0:
                        pe.wait_ge(w_lo, k + 1)
                    for a, w in PASSES:
                        for half in range(2):
                            last = nc.tensor.matmul(py[t % 2][:, half * 512:(half + 1) * 512],
                                                    K.A[a][:, k, t * P:(t + 1) * P], wo[w][:, k, half * 512:(half + 1) * 512],
                                                    start=(n == 0), stop=(n == 3 * KT - 1))
                        n += 1
                last.then_inc(y_ready, 1)
            feed.turn(pe, lambda c: pe.wait_ge(norm.z, TPC * (c + 1)))

        @block.scalar
        def _(act):
            for k in range(KT):
                nc.scalar.activation(K.A[0][:, k, :], K.O[:, k, :], ACT.Copy).then_inc(o_hi, 1)
                act.wait_ge(raw_in[k % 2], 16 * (k // 2 + 1))
                nc.scalar.activation(wo[0][:, k, :], raw[k % 2][:], ACT.Copy).then_inc(w_hi, 1)
            feed.scale(act)

        @block.vector
        def _(dve):
            for k in range(KT):
                dve.wait_ge(o_hi, k + 1)
                nc.vector.tensor_tensor(K.A[1][:, k, :], K.O[:, k, :], K.A[0][:, k, :].bitcast(F32), ALU.subtract).then_inc(o_lo, 1)
                dve.wait_ge(w_hi, k + 1)
                nc.vector.tensor_tensor(wo[1][:, k, :], raw[k % 2][:], wo[0][:, k, :].bitcast(F32), ALU.subtract).then_inc(w_lo, 1)
            norm.start(dve)
            dve.wait_ge(o_lo, KT)
            for t in range(NT + 1):
                if t < NT:
                    dve.wait_ge(y_ready, t + 1)
                    norm.sums(dve, t, Y, src=py[t % 2], freed=y_taken)
                if t >= 1:
                    norm.unit(dve, t - 1, Y)
            for c in range(NCH):
                feed.rest(dve, c)

        @block.gpsimd
        def _(gp):
            norm.pool(gp, Y)


def rope_tables(np):
    half = DH // 2
    inv = 10000.0 ** (-np.arange(0, half, 2, dtype=np.float32) / half)
    n = np.arange(N_LAT)
    row = (n // GRID_W).astype(np.float32)[:, None] * inv
    col = (n % GRID_W).astype(np.float32)[:, None] * inv
    cos = np.concatenate([np.cos(row), np.cos(row), np.cos(col), np.cos(col)], 1)
    sin = np.concatenate([-np.sin(row), np.sin(row), -np.sin(col), np.sin(col)], 1)
    tab = np.stack([np.concatenate([cos, np.ones((N_CTX, DH))]), np.concatenate([sin, np.zeros((N_CTX, DH))])])
    return tab.astype(np.float32)


class Kernel:

    def semaphore(self, name):
        self.held.append(self.nc.alloc_semaphore(name))
        return self.held[-1]

    def clear_semaphores(self):
        self.nc.clear_and_free_semaphores(self.held)
        self.nc.all_engine_barrier()
        self.held = []


def program(nc, K):
    K.nc, K.held = nc, []
    place = Plan(nc, (nc.sbuf_base + 63) // 64 * 64)
    K.ident = place("ident", [P, P])
    K.mod = place("mod_cols", [P, 72, 2])
    K.cols = place("param_cols", [P, C_END])
    K.lbd = place("lb_logit_difference", [P, 2, HGH])
    K.A = [place("act_hi", [P, KT, TOK], F32R), place("act_lo", [P, KT, TOK], F32R)]
    K.o_at = place.at
    K.Y = place("Y", [P, NT, D])
    phase = place.at
    mix = Plan(nc, K.o_at)
    K.O = mix("mix_out_T", [P, KT, TOK])
    mix_at = mix.at
    K.QK = mix("qk_rows", [P, NT, QW + KVW])
    K.V = mix("v_rows", [P, NT, KVW])
    att_at = mix.at
    K.scan_links = 87
    with ExitStack() as ctx:
        psum = ctx.enter_context(nc.psum_tensor("psum", [P, 4096], F32))
        K.score_banks = psum[:, 0:2560]
        K.wide = [psum[:, 1024 * i:1024 * (i + 1)] for i in range(4)]
        banks = [psum[:, 512 * i:512 * (i + 1)] for i in range(8)]
        K.mod_rows = nc.dram_tensor("mod_rows", (2, N_MOD * D), F32).ap()
        x1 = nc.dram_tensor("x_after_1", (TOK, D), F32).ap()
        x2 = nc.dram_tensor("x_after_2", (TOK, D), F32).ap()
        K.x_rows = lambda t: K.x_sample[0, t * P:(t + 1) * P, :] if t < CTX_T else K.x_prompt[0]
        K.x1_rows = lambda t: x1[t * P:(t + 1) * P, :]
        K.x2_rows = lambda t: x2[t * P:(t + 1) * P, :]
        y_rows = lambda t: K.y_sample[0, t * P:(t + 1) * P, :] if t < CTX_T else K.y_prompt[0]
        modulation_phase(nc, K, Plan(nc, phase), banks)
        ffn_phase(nc, K, Plan(nc, phase), banks, "ffn1", K.w1_in, K.w1_out, K.x_rows, K.x1_rows, 2, 0, (4, 3))
        qkv_phase(nc, K, Plan(nc, att_at), banks)
        attention_phase(nc, K, Plan(nc, att_at), banks)
        K.clear_semaphores()
        hgrn_phase(nc, K, Plan(nc, mix_at), banks)
        mix_out_phase(nc, K, Plan(nc, phase), banks)
        ffn_phase(nc, K, Plan(nc, phase), banks, "ffn2", K.w2_in, K.w2_out, K.x2_rows, y_rows, 8, 2, None)


_INS = {"x_prompt": "x_prompt", "x_sample": "x_sample", "cache_k": "cache_k", "cache_v": "cache_v",
        "state_f": "state_hgrn_fwd", "state_b": "state_hgrn_bwd", "c": "c", "c_ctx": "c_ctx",
        "w_mod": "w_mod", "b_mod": "b_mod", "w1_in": "w_ffn1_in", "w1_out": "w_ffn1_out",
        "w2_in": "w_ffn2_in", "w2_out": "w_ffn2_out", "w_mix": "w_in", "w_mix_out": "w_out",
        "q_g": "q_norm_g", "k_g": "k_norm_g", "hg_g": "hg_norm_g", "lb_f": "lb_logits_fwd",
        "lb_b": "lb_logits_bwd", "ln_g": "ln_g", "ln_b": "ln_b"}
_OUTS = {"y_prompt": (1, N_CTX, D), "y_sample": (1, N_LAT, D), "new_k": (1, 1, N_CTX, NKV, DH),
         "new_v": (1, 1, N_CTX, NKV, DH), "new_f": (1, 1, HGH, P, P), "new_b": (1, 1, HGH, P, P)}


def kernel(**inputs):
    import numpy as np
    import concourse.bacc as bacc
    from concourse.bass_utils import run_bass_kernel_spmd as run
    nc = bacc.Bacc("TRN2", target_bir_lowering=False, num_devices=1, dynamic_dma_scratch_size=1024)
    K, arrays = Kernel(), {}

    def declare(attr, array):
        arrays["in_" + attr] = np.ascontiguousarray(array)
        K.__dict__[attr] = nc.dram_tensor("in_" + attr, arrays["in_" + attr].shape, F32, kind="ExternalInput").ap()

    for attr, name in _INS.items():
        declare(attr, inputs[name])
    declare("rope", rope_tables(np))
    for name, shape in _OUTS.items():
        K.__dict__[name] = nc.dram_tensor("out_" + name, shape, F32, kind="ExternalOutput").ap()
    K.ln_g, K.ln_b = K.ln_g[0], K.ln_b[0]
    K.cache_k, K.cache_v = K.cache_k[0, 0], K.cache_v[0, 0]
    K.state_f, K.state_b = K.state_f[0, 0], K.state_b[0, 0]
    K.new_f, K.new_b = K.new_f[0, 0], K.new_b[0, 0]
    K.new_k = K.new_k[0, 0].rearrange("t h d -> t (h d)")
    K.new_v = K.new_v[0, 0].rearrange("t h d -> t (h d)")
    program(nc, K)
    r = run(nc, [arrays], core_ids=[0])
    return tuple(r.results[0]["out_" + name] for name in _OUTS)
```
